# Optimizing a Trainium2 kernel written in Bass

```python
import jax, jax.numpy as jnp
from jax import lax
import numpy as np

D_MODEL = 1024
BATCH = 1
SEQ = 256
DEPTH = 2

GRID_W = 64
CTX_LEN = 256
D_FF = 2816
MIX_W = D_MODEL
A_W = MIX_W // 2
B_W = MIX_W - A_W
GMLP_GROUPS = 4
GMLP_CH = A_W // GMLP_GROUPS
GMLP_CHUNK = 128
HGRN_HEADS = 4
HGRN_K = B_W // HGRN_HEADS
HGRN_V = B_W // HGRN_HEADS
HGRN_CHUNK = 64
IN_W = 2 * A_W + 5 * B_W
N_MOD = 9
EPS = 1e-6
POS_THETA = 10000.0


def _rmsnorm(x, g):
    xf = x.astype(jnp.float32)
    y = xf * lax.rsqrt(jnp.mean(xf * xf, axis=-1, keepdims=True) + EPS)
    return (y * g.astype(jnp.float32)).astype(x.dtype)

def _modulation(cond, w, b):
    m = jax.nn.silu(cond) @ w + b
    return [m[:, None, j * D_MODEL:(j + 1) * D_MODEL] for j in range(N_MOD)]

def _modulate(x, g, shift, scale):
    return _rmsnorm(x, g) * (1 + scale) + shift

def _swiglu(h, w1, w3, w2):
    return (jax.nn.silu(h @ w1) * (h @ w3)) @ w2

def _grid_pos_embed(rows, dtype):
    row = jnp.repeat(jnp.arange(rows), GRID_W).astype(jnp.float32)
    col = jnp.tile(jnp.arange(GRID_W), rows).astype(jnp.float32)
    quarter = D_MODEL // 4
    freq = POS_THETA ** (-jnp.arange(quarter, dtype=jnp.float32) / quarter)

    def axis_embed(p):
        a = p[:, None] * freq[None, :]
        return jnp.concatenate([jnp.sin(a), jnp.cos(a)], axis=-1)

    return jnp.concatenate([axis_embed(row), axis_embed(col)], axis=-1).astype(dtype)

def _gmlp_spatial(u, v, w_s, b_s, g_v):
    B, L, _ = u.shape
    n = L // GMLP_CHUNK
    u = jax.nn.gelu(u).reshape(B, n, GMLP_CHUNK, GMLP_GROUPS, GMLP_CH)
    v = _rmsnorm(jax.nn.gelu(v).reshape(B, L, GMLP_GROUPS, GMLP_CH), g_v.reshape(GMLP_GROUPS, GMLP_CH))
    v = v.reshape(B, n, GMLP_CHUNK, GMLP_GROUPS, GMLP_CH)
    sv = jnp.einsum("gts,bnsgc->bntgc", w_s, v) + b_s.T[:, :, None]
    return (u * sv).reshape(B, L, A_W)

def _lower_bounds(p):
    cum = jnp.cumsum(jax.nn.softmax(p.astype(jnp.float32), axis=0), axis=0)
    return cum - cum[0:1]

def _forget(f_raw, lb):
    f_raw = f_raw.astype(jnp.float32)
    log_f = jnp.logaddexp(jnp.log(lb), jnp.log1p(-lb) + jax.nn.log_sigmoid(f_raw))
    k = (1.0 - lb) * jax.nn.sigmoid(-f_raw)
    return k, log_f

def _gla_scan(q, k, log_f, v, s0):
    B, L, H, K = q.shape
    V = v.shape[-1]
    n = L // HGRN_CHUNK

    def to_chunks(a):
        return a.reshape(B, n, HGRN_CHUNK, H, a.shape[-1]).transpose(1, 0, 3, 2, 4)

    mask = jnp.tril(jnp.ones((HGRN_CHUNK, HGRN_CHUNK), dtype=bool))[:, :, None]

    def step(S, inp):
        qc, kc, gc, vc = inp
        b = jnp.cumsum(gc, axis=2)
        diff = b[:, :, :, None, :] - b[:, :, None, :, :]
        decay = jnp.exp(jnp.where(mask, diff, -jnp.inf))
        scores = jnp.einsum("bhtk,bhsk,bhtsk->bhts", qc, kc, decay)
        o = (jnp.einsum("bhts,bhsv->bhtv", scores, vc)
             + jnp.einsum("bhtk,bhkv->bhtv", qc * jnp.exp(b), S))
        b_end = b[:, :, -1, :]
        S = (jnp.exp(b_end)[..., None] * S
             + jnp.einsum("bhsk,bhsv->bhkv", kc * jnp.exp(b_end[:, :, None, :] - b), vc))
        return S, o

    s_fin, o = lax.scan(step, s0, (to_chunks(q), to_chunks(k), to_chunks(log_f), to_chunks(v)))
    return o.transpose(1, 0, 3, 2, 4).reshape(B, L, H, V), s_fin

def _hgrn_bidir(q, f_fw, f_bw, i, lb_f, lb_b, s0_f, s0_b):
    B, L, _ = q.shape

    def heads(a):
        return a.astype(jnp.float32).reshape(B, L, HGRN_HEADS, -1)

    def flip(a):
        return a[:, ::-1]

    qh = heads(jax.nn.silu(q))
    vh = heads(i)
    kf, gf = _forget(f_fw, lb_f)
    kb, gb = _forget(f_bw, lb_b)
    o_f, s_f = _gla_scan(qh, heads(kf), heads(gf), vh, s0_f)
    o_b, s_b = _gla_scan(flip(qh), flip(heads(kb)), flip(heads(gb)), flip(vh), s0_b)
    return o_f + flip(o_b), s_f, s_b

def _token_mixer(h, w_in, w_out, w_s, b_s, g_v, g_o, lb_f, lb_b, s0_f, s0_b):
    B, L, _ = h.shape
    z = h @ w_in
    cuts = [A_W, 2 * A_W, 2 * A_W + B_W, 2 * A_W + 2 * B_W, 2 * A_W + 3 * B_W, 2 * A_W + 4 * B_W]
    u, v, q, f_fw, f_bw, i, og = jnp.split(z, cuts, axis=-1)
    a_out = _gmlp_spatial(u, v, w_s, b_s, g_v)
    o, s_f, s_b = _hgrn_bidir(q, f_fw, f_bw, i, lb_f, lb_b, s0_f, s0_b)
    o = _rmsnorm(o, g_o.reshape(HGRN_HEADS, HGRN_V)).reshape(B, L, B_W).astype(h.dtype)
    b_out = o * jax.nn.silu(og)
    return jnp.concatenate([a_out, b_out], axis=-1) @ w_out, s_f, s_b

def _context_states(h, w_in, lb_f, lb_b, s0_f, s0_b):
    z = h @ w_in[:, 2 * A_W:2 * A_W + 4 * B_W]
    q, f_fw, f_bw, i = jnp.split(z, 4, axis=-1)
    _, s_f, s_b = _hgrn_bidir(q, f_fw, f_bw, i, lb_f, lb_b, s0_f, s0_b)
    return s_f, s_b

def first_inputs(seed: int = 0) -> dict:
    key = jax.random.key(seed)
    ks = jax.random.split(key, 24)

    def nrm(k, shape, s):
        return jax.random.normal(k, shape, jnp.float32) * s

    def gain(k, shape):
        return 1.0 + 0.02 * jax.random.normal(k, shape, jnp.float32)

    d_s = D_MODEL ** -0.5
    return {
        "x": nrm(ks[0], (BATCH, SEQ, D_MODEL), 1.0),
        "c": nrm(ks[1], (BATCH, D_MODEL), 1.0),
        "ctx": nrm(ks[2], (BATCH, CTX_LEN, D_MODEL), 1.0),
        "c_ctx": nrm(ks[3], (D_MODEL,), 1.0),
        "w_ada": nrm(ks[4], (DEPTH, D_MODEL, N_MOD * D_MODEL), d_s),
        "b_ada": nrm(ks[5], (DEPTH, N_MOD * D_MODEL), 0.02),
        "norm_ffn1_g": gain(ks[6], (DEPTH, D_MODEL)),
        "norm_mix_g": gain(ks[7], (DEPTH, D_MODEL)),
        "norm_ffn2_g": gain(ks[8], (DEPTH, D_MODEL)),
        "ffn1_w1": nrm(ks[9], (DEPTH, D_MODEL, D_FF), d_s),
        "ffn1_w3": nrm(ks[10], (DEPTH, D_MODEL, D_FF), d_s),
        "ffn1_w2": nrm(ks[11], (DEPTH, D_FF, D_MODEL), D_FF ** -0.5),
        "ffn2_w1": nrm(ks[12], (DEPTH, D_MODEL, D_FF), d_s),
        "ffn2_w3": nrm(ks[13], (DEPTH, D_MODEL, D_FF), d_s),
        "ffn2_w2": nrm(ks[14], (DEPTH, D_FF, D_MODEL), D_FF ** -0.5),
        "w_in": nrm(ks[15], (DEPTH, D_MODEL, IN_W), d_s),
        "w_out": nrm(ks[16], (DEPTH, MIX_W, D_MODEL), MIX_W ** -0.5),
        "gmlp_ws": nrm(ks[17], (DEPTH, GMLP_GROUPS, GMLP_CHUNK, GMLP_CHUNK), GMLP_CHUNK ** -0.5),
        "gmlp_bs": gain(ks[18], (DEPTH, GMLP_GROUPS, GMLP_CHUNK)),
        "gmlp_norm_g": gain(ks[19], (DEPTH, A_W)),
        "hgrn_lb_fwd": nrm(ks[20], (DEPTH, B_W), 0.5),
        "hgrn_lb_bwd": nrm(ks[21], (DEPTH, B_W), 0.5),
        "hgrn_norm_g": gain(ks[22], (DEPTH, B_W)),
        "norm_final_g": gain(ks[23], (D_MODEL,)),
    }

def first_block(x, c, ctx, c_ctx, w_ada, b_ada, norm_ffn1_g, norm_mix_g, norm_ffn2_g,
              ffn1_w1, ffn1_w3, ffn1_w2, ffn2_w1, ffn2_w3, ffn2_w2, w_in, w_out,
              gmlp_ws, gmlp_bs, gmlp_norm_g, hgrn_lb_fwd, hgrn_lb_bwd, hgrn_norm_g, norm_final_g):
    B, L, _ = x.shape
    rows = L // GRID_W
    lat = x + _grid_pos_embed(rows, x.dtype)[None]
    cx = ctx
    lbs_f = _lower_bounds(hgrn_lb_fwd)
    lbs_b = _lower_bounds(hgrn_lb_bwd)
    zero_state = jnp.zeros((B, HGRN_HEADS, HGRN_K, HGRN_V), jnp.float32)

    for l in range(DEPTH):
        last = l == DEPTH - 1
        ml = _modulation(c, w_ada[l], b_ada[l])
        mc = _modulation(c_ctx[None], w_ada[l], b_ada[l])

        ffn1 = (ffn1_w1[l], ffn1_w3[l], ffn1_w2[l])
        lat = lat + 0.5 * ml[2] * _swiglu(_modulate(lat, norm_ffn1_g[l], ml[0], ml[1]), *ffn1)
        cx = cx + 0.5 * mc[2] * _swiglu(_modulate(cx, norm_ffn1_g[l], mc[0], mc[1]), *ffn1)

        mix_w = (w_in[l], w_out[l], gmlp_ws[l], gmlp_bs[l], gmlp_norm_g[l], hgrn_norm_g[l],
                 lbs_f[l], lbs_b[l])
        h_cx = _modulate(cx, norm_mix_g[l], mc[3], mc[4])
        if last:
            s_f, s_b = _context_states(h_cx, w_in[l], lbs_f[l], lbs_b[l], zero_state, zero_state)
        else:
            out_cx, s_f, s_b = _token_mixer(h_cx, *mix_w, zero_state, zero_state)
            cx = cx + mc[5] * out_cx
        out_lat, _, _ = _token_mixer(_modulate(lat, norm_mix_g[l], ml[3], ml[4]), *mix_w, s_f, s_b)
        lat = lat + ml[5] * out_lat

        ffn2 = (ffn2_w1[l], ffn2_w3[l], ffn2_w2[l])
        lat = lat + 0.5 * ml[8] * _swiglu(_modulate(lat, norm_ffn2_g[l], ml[6], ml[7]), *ffn2)
        if not last:
            cx = cx + 0.5 * mc[8] * _swiglu(_modulate(cx, norm_ffn2_g[l], mc[6], mc[7]), *ffn2)

    return _rmsnorm(lat, norm_final_g)


_first_inputs = first_inputs


def first_inputs(seed=0):
    import zlib

    import numpy as np

    out = dict(_first_inputs(seed))
    spreads = {}
    factors = {'ctx': 6.378,
     'c_ctx': 4.813,
     'norm_ffn1_g': 5.796,
     'norm_mix_g': 3.902,
     'norm_ffn2_g': 6.896,
     'gmlp_bs': 7.398,
     'gmlp_norm_g': 7.631,
     'hgrn_lb_fwd': 8.0,
     'hgrn_lb_bwd': 8.0,
     'hgrn_norm_g': 7.333,
     'norm_final_g': 2.876}
    for name, (base, spread) in spreads.items():
        noise = np.random.default_rng([zlib.crc32(name.encode()), seed]).standard_normal(out[name].shape)
        drawn = base * np.exp(spread * noise) if base else spread * noise
        out[name] = __import__('jax').numpy.asarray(drawn.astype(out[name].dtype))
    for name, factor in factors.items():
        out[name] = (out[name] * factor).astype(out[name].dtype)
    return out


_narrow_inputs = first_inputs


def first_inputs(seed=0):
    out = dict(_narrow_inputs(seed))
    wider = {'gmlp_bs': 4.12, 'gmlp_norm_g': 3.88, 'hgrn_norm_g': 3.84, 'norm_final_g': 3.18}
    for name, times in wider.items():
        mean = out[name].mean()
        out[name] = (mean + times * (out[name] - mean)).astype(out[name].dtype)
    return out


DEPTH_2 = 1

N_MEM = 256

HEAD_DIM = 64
DIL_PATTERNS = ((128, 1), (512, 4), (2048, 16))
N_GROUPS = len(DIL_PATTERNS)
ATTN_SLOTS = 4
ATTN_HEADS = N_GROUPS * ATTN_SLOTS
ATTN_WIDTH = ATTN_HEADS * HEAD_DIM
ATTN_OUT = ATTN_SLOTS * HEAD_DIM
ROT_DIM = HEAD_DIM // 4
ROPE_THETA = 500000.0

CONV_WIDTH = 768
CONV_K = 3

MEM_HEADS = 4
MEM_HEAD_DIM = 128
MEM_WIDTH = MEM_HEADS * MEM_HEAD_DIM

N_BRANCH = 3
IN_SIZES = (ATTN_WIDTH, ATTN_WIDTH, ATTN_WIDTH, CONV_WIDTH, CONV_WIDTH, CONV_WIDTH,
            MEM_WIDTH, N_BRANCH * D_MODEL)
IN_COLS = sum(IN_SIZES)
IN_SPLITS = tuple(int(c) for c in np.cumsum(IN_SIZES)[:-1])

N_EXPERT_GROUPS = 4
EXPERTS_PER_GROUP = 8
N_EXPERTS = N_EXPERT_GROUPS * EXPERTS_PER_GROUP
TOP_K = 2
EXPERT_FF = 512
MOE_BLOCK = 256


def _rmsnorm_2(x, g):
    xf = x.astype(jnp.float32)
    y = xf * lax.rsqrt(jnp.mean(xf * xf, axis=-1, keepdims=True) + EPS)
    return (y * g.astype(jnp.float32)).astype(x.dtype)

def _rope_tables(positions):
    inv = ROPE_THETA ** (-jnp.arange(0, ROT_DIM, 2, dtype=jnp.float32) / ROT_DIM)
    ang = positions.astype(jnp.float32)[..., None] * inv
    return jnp.cos(ang)[:, :, None, :], jnp.sin(ang)[:, :, None, :]

def _partial_rope(t, cos, sin):
    tr = t[..., :ROT_DIM].astype(jnp.float32)
    t1, t2 = tr[..., :ROT_DIM // 2], tr[..., ROT_DIM // 2:]
    rot = jnp.concatenate([t1 * cos - t2 * sin, t2 * cos + t1 * sin], axis=-1)
    return jnp.concatenate([rot.astype(t.dtype), t[..., ROT_DIM:]], axis=-1)

def _banded_attention(q, k, v, half):
    b, g, L, h, dh = q.shape
    blk = half
    nb = -(-L // blk)
    lp = nb * blk
    qb = jnp.pad(q, ((0, 0), (0, 0), (0, lp - L), (0, 0), (0, 0))).reshape(b, g, nb, blk, h, dh)
    pad_k = ((0, 0), (0, 0), (blk, lp - L + blk), (0, 0), (0, 0))

    def windows(t):
        tb = jnp.pad(t, pad_k).reshape(b, g, nb + 2, blk, h, dh)
        return jnp.concatenate([tb[:, :, :-2], tb[:, :, 1:-1], tb[:, :, 2:]], axis=3)

    kw, vw = windows(k), windows(v)
    qpos = np.arange(nb)[:, None] * blk + np.arange(blk)[None, :]
    kpos = np.arange(nb)[:, None] * blk - blk + np.arange(3 * blk)[None, :]
    valid = ((np.abs(qpos[:, :, None] - kpos[:, None, :]) <= half)
             & (kpos[:, None, :] >= 0) & (kpos[:, None, :] < L))
    s = jnp.einsum('bgnqhd,bgnkhd->bgnhqk', qb, kw).astype(jnp.float32) * (dh ** -0.5)
    s = jnp.where(jnp.asarray(valid)[:, None], s, jnp.finfo(jnp.float32).min)
    m = jnp.max(s, axis=-1, keepdims=True)
    p = jnp.exp(s - m)
    den = jnp.sum(p, axis=-1)
    o = jnp.einsum('bgnhqk,bgnkhd->bgnqhd', p.astype(v.dtype), vw)
    o = o / jnp.transpose(den, (0, 1, 2, 4, 3))[..., None].astype(o.dtype)
    lse = jnp.transpose(m[..., 0] + jnp.log(den), (0, 1, 2, 4, 3))
    o = o.reshape(b, g, lp, h, dh)[:, :, :L]
    lse = lse.reshape(b, g, lp, h)[:, :, :L]
    return o, lse

def _dilated_attention(q, k, v, window, dilation):
    b, s, h, dh = q.shape
    L = s // dilation
    half = window // (2 * dilation)

    def to_sub(t):
        return jnp.transpose(t.reshape(b, L, dilation, h, dh), (0, 2, 1, 3, 4))

    o, lse = _banded_attention(to_sub(q), to_sub(k), to_sub(v), half)
    o = jnp.transpose(o, (0, 2, 1, 3, 4)).reshape(b, s, h, dh)
    lse = jnp.transpose(lse, (0, 2, 1, 3)).reshape(b, s, h)
    return o, lse

def _hierarchical_moe(h, w_rg, b_rg, w_re, b_re, w_gate, w_up, w_down):
    b, s, d = h.shape
    n = b * s
    hf = h.reshape(n, d)
    hr = hf.astype(jnp.float32)
    pg = jax.nn.softmax(hr @ w_rg.astype(jnp.float32) + b_rg.astype(jnp.float32), axis=-1)
    pg_top, g_idx = lax.top_k(pg, 1)
    el = (hr @ w_re.astype(jnp.float32) + b_re.astype(jnp.float32)).reshape(n, N_EXPERT_GROUPS, EXPERTS_PER_GROUP)
    sel = jnp.einsum('ng,nge->ne', jax.nn.one_hot(g_idx[:, 0], N_EXPERT_GROUPS, dtype=jnp.float32), el)
    pe_top, e_idx = lax.top_k(jax.nn.softmax(sel, axis=-1), TOP_K)
    weights = pg_top * pe_top / jnp.sum(pe_top, axis=-1, keepdims=True)
    ids = g_idx * EXPERTS_PER_GROUP + e_idx

    nk = n * TOP_K
    e = ids.reshape(nk).astype(jnp.int32)
    w = weights.reshape(nk)
    t = jnp.repeat(jnp.arange(n, dtype=jnp.int32), TOP_K)
    order = jnp.argsort(e, stable=True)
    e_s, t_s, w_s = e[order], t[order], w[order]
    counts = jnp.bincount(e, length=N_EXPERTS)
    padded = ((counts + MOE_BLOCK - 1) // MOE_BLOCK) * MOE_BLOCK
    start = jnp.cumsum(counts) - counts
    pend = jnp.cumsum(padded)
    pstart = pend - padded
    dest = pstart[e_s] + (jnp.arange(nk, dtype=jnp.int32) - start[e_s])
    n_rows = (-(-nk // MOE_BLOCK) + N_EXPERTS) * MOE_BLOCK
    n_blk = n_rows // MOE_BLOCK
    row_tok = jnp.zeros((n_rows,), jnp.int32).at[dest].set(t_s)
    row_w = jnp.zeros((n_rows,), jnp.float32).at[dest].set(w_s)
    blk_exp = jnp.minimum(jnp.searchsorted(pend, jnp.arange(n_blk) * MOE_BLOCK, side='right'),
                          N_EXPERTS - 1).astype(jnp.int32)

    def expert_block(args):
        tok, wt, ex = args
        xb = hf[tok]
        a = xb @ w_gate[ex]
        u = xb @ w_up[ex]
        y = (jax.nn.silu(a) * u) @ w_down[ex]
        return y * wt[:, None].astype(y.dtype)

    ys = lax.map(expert_block, (row_tok.reshape(n_blk, MOE_BLOCK),
                                row_w.reshape(n_blk, MOE_BLOCK), blk_exp))
    out = jnp.zeros((n, d), h.dtype).at[row_tok].add(ys.reshape(n_rows, d).astype(h.dtype))
    return out.reshape(b, s, d)

def second_inputs(seed: int = 0) -> dict:
    key = jax.random.key(seed)
    ks = jax.random.split(key, 24)
    f32 = jnp.float32

    def nrm(k, shape, scale):
        return jax.random.normal(k, shape, f32) * scale

    def gain(k, dim):
        return 1.0 + 0.05 * jax.random.normal(k, (DEPTH_2, dim), f32)

    x = jax.random.normal(ks[0], (BATCH, SEQ, D_MODEL), f32)
    mem = jax.random.normal(ks[1], (BATCH, N_MEM, D_MODEL), f32)
    positions = (jnp.arange(SEQ, dtype=jnp.int32)[None, :]
                 + jax.random.randint(ks[2], (BATCH, 1), 0, 4096, dtype=jnp.int32))
    return {
        'x': x,
        'mem': mem,
        'positions': positions,
        'g_mix': gain(ks[3], D_MODEL),
        'g_mem': gain(ks[4], D_MODEL),
        'w_in': nrm(ks[5], (DEPTH_2, D_MODEL, IN_COLS), D_MODEL ** -0.5),
        'g_qn_attn': gain(ks[6], HEAD_DIM),
        'g_kn_attn': gain(ks[7], HEAD_DIM),
        'w_conv': nrm(ks[8], (DEPTH_2, CONV_K, CONV_WIDTH), CONV_K ** -0.5),
        'w_mem_kv': nrm(ks[9], (DEPTH_2, D_MODEL, 2 * MEM_WIDTH), D_MODEL ** -0.5),
        'g_qn_mem': gain(ks[10], MEM_HEAD_DIM),
        'g_kn_mem': gain(ks[11], MEM_HEAD_DIM),
        'w_proj_attn': nrm(ks[12], (DEPTH_2, ATTN_OUT, D_MODEL), ATTN_OUT ** -0.5),
        'w_proj_conv': nrm(ks[13], (DEPTH_2, CONV_WIDTH, D_MODEL), CONV_WIDTH ** -0.5),
        'w_proj_mem': nrm(ks[14], (DEPTH_2, MEM_WIDTH, D_MODEL), MEM_WIDTH ** -0.5),
        'w_out': nrm(ks[15], (DEPTH_2, D_MODEL, D_MODEL), D_MODEL ** -0.5),
        'g_ffn': gain(ks[16], D_MODEL),
        'w_router_group': nrm(ks[17], (DEPTH_2, D_MODEL, N_EXPERT_GROUPS), D_MODEL ** -0.5),
        'b_router_group': nrm(ks[18], (DEPTH_2, N_EXPERT_GROUPS), 0.01),
        'w_router_expert': nrm(ks[19], (DEPTH_2, D_MODEL, N_EXPERTS), D_MODEL ** -0.5),
        'b_router_expert': nrm(ks[20], (DEPTH_2, N_EXPERTS), 0.01),
        'w_gate': nrm(ks[21], (DEPTH_2, N_EXPERTS, D_MODEL, EXPERT_FF), D_MODEL ** -0.5),
        'w_up': nrm(ks[22], (DEPTH_2, N_EXPERTS, D_MODEL, EXPERT_FF), D_MODEL ** -0.5),
        'w_down': nrm(ks[23], (DEPTH_2, N_EXPERTS, EXPERT_FF, D_MODEL), EXPERT_FF ** -0.5),
    }

def second_block(x, mem, positions, g_mix, g_mem, w_in, g_qn_attn, g_kn_attn, w_conv,
              w_mem_kv, g_qn_mem, g_kn_mem, w_proj_attn, w_proj_conv, w_proj_mem, w_out,
              g_ffn, w_router_group, b_router_group, w_router_expert, b_router_expert,
              w_gate, w_up, w_down):
    b, s, d = x.shape
    cos, sin = _rope_tables(positions)
    cos, sin = cos.astype(x.dtype), sin.astype(x.dtype)
    for l in range(DEPTH_2):
        h = _rmsnorm_2(x, g_mix[l])
        proj = h @ w_in[l]
        q_a, k_a, v_a, cx, cb, cc, q_m, gate_logits = jnp.split(proj, IN_SPLITS, axis=-1)

        q_a = _partial_rope(_rmsnorm_2(q_a.reshape(b, s, ATTN_HEADS, HEAD_DIM), g_qn_attn[l]), cos, sin)
        k_a = _partial_rope(_rmsnorm_2(k_a.reshape(b, s, ATTN_HEADS, HEAD_DIM), g_kn_attn[l]), cos, sin)
        v_a = v_a.reshape(b, s, ATTN_HEADS, HEAD_DIM)
        q_a = q_a.reshape(b, s, N_GROUPS, ATTN_SLOTS, HEAD_DIM)
        k_a = k_a.reshape(b, s, N_GROUPS, ATTN_SLOTS, HEAD_DIM)
        v_a = v_a.reshape(b, s, N_GROUPS, ATTN_SLOTS, HEAD_DIM)
        outs, lses = [], []
        for gi, (window, dilation) in enumerate(DIL_PATTERNS):
            o_g, lse_g = _dilated_attention(q_a[:, :, gi], k_a[:, :, gi], v_a[:, :, gi], window, dilation)
            outs.append(o_g)
            lses.append(lse_g)
        alpha = jax.nn.softmax(jnp.stack(lses, axis=2), axis=2)
        o_attn = jnp.einsum('bsgh,bsghd->bshd', alpha.astype(x.dtype),
                            jnp.stack(outs, axis=2)).reshape(b, s, ATTN_OUT)

        u = cc * cx
        up = jnp.pad(u, ((0, 0), (1, 1), (0, 0)))
        wc = w_conv[l]
        y_conv = wc[0] * up[:, :-2] + wc[1] * up[:, 1:-1] + wc[2] * up[:, 2:]
        z_conv = cb * y_conv

        mkv = _rmsnorm_2(mem, g_mem[l]) @ w_mem_kv[l]
        k_m, v_m = jnp.split(mkv, 2, axis=-1)
        k_m = _rmsnorm_2(k_m.reshape(b, N_MEM, MEM_HEADS, MEM_HEAD_DIM), g_kn_mem[l])
        v_m = v_m.reshape(b, N_MEM, MEM_HEADS, MEM_HEAD_DIM)
        q_m = _rmsnorm_2(q_m.reshape(b, s, MEM_HEADS, MEM_HEAD_DIM), g_qn_mem[l])
        sm = jnp.einsum('bshd,bmhd->bhsm', q_m, k_m).astype(jnp.float32) * (MEM_HEAD_DIM ** -0.5)
        pm = jax.nn.softmax(sm, axis=-1).astype(v_m.dtype)
        o_mem = jnp.einsum('bhsm,bmhd->bshd', pm, v_m).reshape(b, s, MEM_WIDTH)

        gates = jax.nn.sigmoid(gate_logits).reshape(b, s, N_BRANCH, d)
        merged = (gates[:, :, 0] * (o_attn @ w_proj_attn[l])
                  + gates[:, :, 1] * (z_conv @ w_proj_conv[l])
                  + gates[:, :, 2] * (o_mem @ w_proj_mem[l]))
        x = x + merged @ w_out[l]

        h2 = _rmsnorm_2(x, g_ffn[l])
        x = x + _hierarchical_moe(h2, w_router_group[l], b_router_group[l], w_router_expert[l],
                                  b_router_expert[l], w_gate[l], w_up[l], w_down[l])
    return x


def setup_inputs(seed=0):
    out = dict(first_inputs(seed))
    for name, value in second_inputs(seed + 1).items():
        if name != "x":
            out[name + "_2"] = value
    return out


def reference(
    x, c, ctx, c_ctx, w_ada, b_ada, norm_ffn1_g, norm_mix_g, norm_ffn2_g, ffn1_w1, ffn1_w3,
    ffn1_w2, ffn2_w1, ffn2_w3, ffn2_w2, w_in, w_out, gmlp_ws, gmlp_bs, gmlp_norm_g, hgrn_lb_fwd,
    hgrn_lb_bwd, hgrn_norm_g, norm_final_g, mem_2, positions_2, g_mix_2, g_mem_2, w_in_2,
    g_qn_attn_2, g_kn_attn_2, w_conv_2, w_mem_kv_2, g_qn_mem_2, g_kn_mem_2, w_proj_attn_2,
    w_proj_conv_2, w_proj_mem_2, w_out_2, g_ffn_2, w_router_group_2, b_router_group_2,
    w_router_expert_2, b_router_expert_2, w_gate_2, w_up_2, w_down_2,
):
    x = first_block(
        x, c, ctx, c_ctx, w_ada, b_ada, norm_ffn1_g, norm_mix_g, norm_ffn2_g, ffn1_w1, ffn1_w3,
        ffn1_w2, ffn2_w1, ffn2_w3, ffn2_w2, w_in, w_out, gmlp_ws, gmlp_bs, gmlp_norm_g,
        hgrn_lb_fwd, hgrn_lb_bwd, hgrn_norm_g, norm_final_g,
    )
    return second_block(
        x, mem_2, positions_2, g_mix_2, g_mem_2, w_in_2, g_qn_attn_2, g_kn_attn_2, w_conv_2,
        w_mem_kv_2, g_qn_mem_2, g_kn_mem_2, w_proj_attn_2, w_proj_conv_2, w_proj_mem_2, w_out_2,
        g_ffn_2, w_router_group_2, b_router_group_2, w_router_expert_2, b_router_expert_2,
        w_gate_2, w_up_2, w_down_2,
    )


_drawn_inputs = setup_inputs


def setup_inputs(seed=0):
    import zlib

    import numpy as np

    out = dict(_drawn_inputs(seed))
    spreads = {}
    factors = {'g_mix_2': 3.105,
     'g_mem_2': 8.0,
     'g_qn_attn_2': 8.0,
     'g_kn_attn_2': 8.0,
     'g_qn_mem_2': 8.0,
     'g_kn_mem_2': 8.0,
     'g_ffn_2': 2.985,
     'b_router_group_2': 17.182,
     'b_router_expert_2': 24.445}
    for name, (base, spread) in spreads.items():
        noise = np.random.default_rng([zlib.crc32(name.encode()), seed]).standard_normal(out[name].shape)
        drawn = base * np.exp(spread * noise) if base else spread * noise
        out[name] = __import__('jax').numpy.asarray(drawn.astype(out[name].dtype))
    for name, factor in factors.items():
        out[name] = (out[name] * factor).astype(out[name].dtype)
    return out
```

```python
from contextlib import ExitStack, contextmanager

import numpy as np
import concourse.bass as bass
from concourse import mybir

F32 = mybir.dt.float32
I32 = mybir.dt.int32
ALU = mybir.AluOpType
ACT = mybir.ActivationFunctionType
AX = mybir.AxisListType.X

P = 128
D = 1024
KD = D // P
L = 256
T2 = 2 * L
FF = 2816
KF = FF // P
DEPTH = 2
N_MOD = 9
HEADS = 4
EPS = 1e-6
SLOTS = 4
SLAB = KD * 256
W2K = (6, 6, 5, 5)
LEVELS = 7
N_EXP = 32
EXP_FF = 512
AH = 12
CONV_W = 768
NEG = -1e30
WORK = 24064
TWO_PI = 6.283185307179586
PI_1 = 6.28125
PI_2 = 0.0019350051879882812
PI_3 = TWO_PI - PI_1 - PI_2
PI_MAX = 3.1415925
ROUND = 12582912.0
WORK = 24064
TWO_PI = 6.283185307179586
PI_1 = 6.28125
PI_2 = 0.0019350051879882812
PI_3 = TWO_PI - PI_1 - PI_2
PI_MAX = 3.1415925
ROUND = 12582912.0
WORK = 24064
TWO_PI = 6.283185307179586
PI_1 = 6.28125
PI_2 = 0.0019350051879882812
PI_3 = TWO_PI - PI_1 - PI_2
PI_MAX = 3.1415925
ROUND = 12582912.0
WORK = 24064
TWO_PI = 6.283185307179586
PI_1 = 6.28125
PI_2 = 0.0019350051879882812
PI_3 = TWO_PI - PI_1 - PI_2
PI_MAX = 3.1415925
ROUND = 12582912.0
WORK = 24064
TWO_PI = 6.283185307179586
PI_1 = 6.28125
PI_2 = 0.0019350051879882812
PI_3 = TWO_PI - PI_1 - PI_2
PI_MAX = 3.1415925
ROUND = 12582912.0

VEC = {}
_n = 0
for _name, _w in (("b_ada", DEPTH * N_MOD * KD), ("g_norm", DEPTH * 3 * KD), ("g_gmlp", DEPTH * 4), ("lb", 2 * DEPTH * 4),
                  ("g_hgrn", DEPTH * 4), ("g_final", KD), ("g_mix", KD), ("g_mem", KD), ("g_qa", 1), ("g_ka", 1),
                  ("w_conv", 3 * 6), ("g_qm", 1), ("g_km", 1), ("g_ffn", KD), ("inv", 1)):
    VEC[_name] = (_n, _n + _w)
    _n += _w
N_VEC = _n


class Tally:

    def __init__(self):
        self.n, self.step, self.i = 0, 0, None

    def now(self, back=0):
        return self.n - back if self.i is None else self.i * self.step + (self.n - back)


class Side:

    def __init__(self, eng):
        self.eng, self.seen = eng, {}

    def tally(self, sem):
        if sem not in self.seen:
            self.seen[sem] = Tally()
        return self.seen[sem]

    def count(self, sem, k=1):
        self.tally(sem).n += k

    def wait(self, sem, k=1):
        self.count(sem, k)
        self.eng.wait_ge(sem, self.tally(sem).now())

    @contextmanager
    def loop(self, trips, steps):
        before = {}
        with self.eng.Fori(0, trips) as i:
            for sem, k in steps.items():
                t = self.tally(sem)
                before[sem] = t.n
                t.step, t.i = k, i
            yield i
        for sem, k in steps.items():
            t = self.seen[sem]
            assert t.n == before[sem] + k, (sem, t.n - before[sem], k)
            t.n, t.step, t.i = before[sem] + k * trips, 0, None


def build(nc, a, out):
    with ExitStack() as ctx:
        def sb(name, shape, dt=F32):
            return ctx.enter_context(nc.sbuf_tensor(name, shape, dt))

        def sem(name):
            return ctx.enter_context(nc.semaphore(name))

        x = sb("x", [P, KD, T2])
        h = sb("h", [P, KD, T2])
        ring = sb("ring", [P, SLOTS, SLAB])
        rs = sb("rs", [P, T2])
        vec = sb("vec", [P, N_VEC])
        ident = sb("ident", [P, P])
        ones = sb("ones", [P, P])
        zero = sb("zero", [P, P])
        cvec = sb("cvec", [P, KD, 2])
        mod = sb("mod", [P, N_MOD * KD, 2])
        gmod = sb("gmod", [P, 3, KD, 2])
        glamask = sb("glamask", [P, 2 * 8 * P])
        pmt = sb("pmt", [P, 2 * 8 * P])
        kt = sb("kt", [P, 3, P])
        st = sb("st", [P, 3, P])
        keep = sb("keep", [P, T2])
        ws = sb("ws", [P, DEPTH, 4, P])
        bs = sb("bs", [P, DEPTH, 4, P])
        be = sb("be", [P, 2, 4])
        eb = sb("eb", [P, 2, 4])
        lb1 = sb("lb1", [P, 4, 2, 4])
        vms = sb("vms", [P, 16])
        blk64 = sb("blk64", [P, P])
        rot = sb("rot", [P, P])
        amask = sb("amask", [P, 2, 3 * L])
        rw = sb("rw", [P, KD, 36])
        rb = sb("rb", [P, 36 + 8])
        posi = sb("posi", [P, L], I32)
        cosn = sb("cosn", [P, L])
        sinn = sb("sinn", [P, L])
        work = sb("work", [P, WORK])
        ps = ctx.enter_context(nc.psum_tensor("ps", [P, 8, 512], F32))
        psf = ps[:].rearrange("p b n -> p (b n)")

        off = [0]

        def shaped(v, *shape):
            names = "abcd"[:len(shape)]
            return v if len(shape) == 1 else v.rearrange(
                f"p ({' '.join(names)}) -> p {' '.join(names)}", **dict(zip(names, shape)))

        def part(*shape):
            n = int(np.prod(shape))
            off[0] += n
            assert off[0] <= WORK, off[0]
            return shaped(work[:, off[0] - n:off[0]], *shape)

        hid = part(KF, T2)
        sil = part(2, 2, T2)
        off[0] = 0
        lf = part(2, 4, T2)
        kk = part(2, 4, T2)
        vi = part(4, 512)
        qq = part(4, T2)
        og = part(4, T2)
        ex = part(2, LEVELS + 2, T2)
        bb = part(T2)
        gt1, uu = ex[:, 0, 0:4, :], ex[:, 0, 4:8, :]
        gt2, vg = ex[:, 1, 0:4, :], ex[:, 1, 4:8, :]
        off[0] = 0
        qk = part(AH, L)
        km = part(4, L)
        qm = part(4, L)
        kqm = shaped(work[:, 12 * L:20 * L], 8, L)
        va = part(2, 768)
        vm = part(2, 512)
        at = off[0]
        cx = part(3, 6, L)
        mg = part(KD, L)
        t3 = shaped(work[:, at:at + AH * L], AH, L)
        t4 = shaped(work[:, at + AH * L:at + 2 * AH * L], AH, L)
        gt = part(24, L)
        oa = part(2, L)
        zc = part(6, L)
        om = part(4, L)
        memx = gt[:, 0:KD, :]
        off[0] = 0
        wb = part(N_EXP, L)
        gu = part(2, 4, L)
        su = part(2, 2, L)
        tt2 = part(2, 2, L)
        lg = part(2, 36)
        ra = part(12, 2, 8)
        rwt = part(2, 32)
        pm = shaped(pmt[:], 2, 8, P)
        gm = shaped(glamask[:], 2, 8, P)
        sc = shaped(pmt[:, 0:2 * 3 * L], 2, 3 * L)
        pt = shaped(glamask[:, 0:2 * 3 * L], 2, 3 * L)
        dg = shaped(pmt[:, 0:1024], 2, 4, P)

        slot_full = [sem(f"slot_full{i}") for i in range(SLOTS)]
        const_in = sem("const_in")
        mem_in = sem("mem_in")
        out_in = sem("out_in")
        slab_done = sem("slab_done")
        drained = sem("drained")
        silu_c = sem("silu_c")
        start_d = sem("start_d")
        start_a = sem("start_a")
        zeroed = sem("zeroed")
        silu_done = sem("silu_done")
        mod_done = sem("mod_done")
        sq_done = sem("sq_done")
        ssq_done = sem("ssq_done")
        inv_done = sem("inv_done")
        rs_done = sem("rs_done")
        xh_done = sem("xh_done")
        h_done = sem("h_done")
        act_own = sem("act_own")
        dve_own = sem("dve_own")
        gate_a = sem("gate_a")
        gate_d = sem("gate_d")
        gm_ms = sem("gm_ms")
        gm_rs = sem("gm_rs")
        gm_v = sem("gm_v")
        gm_sv = sem("gm_sv")
        gm_out = sem("gm_out")
        dec_in = sem("dec_in")
        dec_out = sem("dec_out")
        xq_done = sem("xq_done")
        xk_done = sem("xk_done")
        ktp_done = sem("ktp_done")
        kt_done = sem("kt_done")
        kv_done = sem("kv_done")
        st_done = sem("st_done")
        sc_done = sem("sc_done")
        pm_done = sem("pm_done")
        pv_done = sem("pv_done")
        hd_done = sem("hd_done")
        o_out = sem("o_out")
        bo_done = sem("bo_done")
        conv_done = sem("conv_done")
        att_a = sem("att_a")
        att_d = sem("att_d")
        att_p = sem("att_p")
        un_sc = sem("un_sc")
        un_mx = sem("un_mx")
        un_ex = sem("un_ex")
        un_pr = sem("un_pr")
        un_tp = sem("un_tp")
        un_pt = sem("un_pt")
        un_o = sem("un_o")
        un_out = sem("un_out")
        rt_p = sem("rt_p")
        rt_d = sem("rt_d")
        rt_a = sem("rt_a")
        rt_dg = sem("rt_dg")
        rt_bc = sem("rt_bc")
        rt_wb = sem("rt_wb")
        moe_s = sem("moe_s")
        moe_gu = sem("moe_gu")
        fin = sem("fin")
        N_CONST = 18

        def v(name, i0=0, n=1):
            c = VEC[name][0] + i0
            return vec[:, c:c + n]

        def halves(n):
            return [(0, slice(0, L)), (1, slice(L, T2))][:n // L]

        def early_late(view, d):
            return view[:, :, d, :], view[:, :, 1 - d, :]

        def blocks(view, m):
            return view.rearrange("p (n two m) -> p n two m", two=2, m=m)

        seq = ([2, 3, 0, 1], [3, 2, 1, 0])
        units = [("a", s, t) for s in range(4) for t in range(2)] + [("m", s, t) for s in range(4) for t in range(2)]

        block = ctx.enter_context(nc.Block())

        @block.sync
        def _(sp):
            S = Side(sp)
            sent = Tally()

            def send(src, width):
                n = sent.n
                if n >= SLOTS:
                    sp.wait_ge(slab_done, sent.now(SLOTS - 1))
                sp.dma_start(ring[:, n % SLOTS, 0:width], src).then_inc(slot_full[n % SLOTS], 16)
                sent.n += 1

            def stream(arr, first, count, width=SLAB):
                trips, rest = divmod(count, SLOTS)
                if sent.n == 0:
                    for j in range(SLOTS):
                        send(arr[first + j], width)
                    first, trips = first + SLOTS, trips - 1
                if trips > 1:
                    n0 = sent.n
                    with sp.Fori(0, trips) as i:
                        sent.step, sent.i = SLOTS, i
                        for j in range(SLOTS):
                            send(arr[i * SLOTS + (first + j)], width)
                    sent.n, sent.step, sent.i = n0 + trips * SLOTS, 0, None
                    first += trips * SLOTS
                    trips = 0
                for j in range(trips * SLOTS + rest):
                    send(arr[first + j], width)

            def ffn(f):
                stream(a["w13"], f * 22, 22)
                for pair in range(4):
                    k0 = 0
                    for k in W2K:
                        send(a["w2"][f * 4 + pair, :, k0 * 256:(k0 + k) * 256], k * 256)
                        k0 += k

            for l in range(DEPTH):
                stream(a["w_ada"], l * 36, 36)
                ffn(2 * l)
                stream(a["w_in"], l * 14, 14)
                stream(a["w_out"], l * 4, 4)
                ffn(2 * l + 1)
            sp.wait_ge(slab_done, sent.now())
            sp.dma_start(memx, a["memx"]).then_inc(mem_in, 16)
            stream(a["w_mem"], 0, 4)
            stream(a["w_in2"], 0, 32)
            stream(a["w_pa"], 0, 4, 2 * 256)
            stream(a["w_pc"], 0, 4, 6 * 256)
            stream(a["w_pm"], 0, 4, 4 * 256)
            stream(a["w_out2"], 0, 4)
            stream(a["w_moe"], 0, 6 * N_EXP)
            S.wait(fin)
            n = 1
            sp.dma_start(out, x[:, :, 0:L]).then_inc(out_in, 16)
            sp.wait_ge(out_in, 16 * n)

        def second(pe, S, chans, tokens, all_drained, norm, slabs, take, slab):
            norm(L)
            S.count(xh_done, 7 * KD)
            norm(L)
            for j in range(2):
                chans(lambda k: h[:, k, 0:L], KD, L, xh_done if j == 0 else None)
            for j in range(2):
                tokens(lambda k, t: h[:, k, t * P:t * P + P], 2)
            norm(L)
            for j in range(20):
                if 15 <= j < 18:
                    tokens(lambda k, t: h[:, k, t * P:t * P + P], 2)
                else:
                    chans(lambda k: h[:, k, 0:L], KD, L, xh_done if j == 0 else None)
            with slabs(3, 4):
                for j in range(4):
                    chans(lambda k: h[:, k, 0:L], KD, L)
            all_drained()
            S.wait(att_a)
            for b in range(6):
                last = nc.tensor.matmul(ps[:, b, :], blk64[:], t3[:, 2 * b:2 * b + 2, :], start=True, stop=True)
            last.then_inc(att_p, 1)
            S.wait(att_d, 2)
            for b in range(6):
                last = nc.tensor.matmul(ps[:, b, :], rot[:], qk[:, 2 * b:2 * b + 2, :], start=True, stop=True)
            last.then_inc(att_p, 1)
            S.wait(att_d)
            S.wait(att_a, 2)
            for b in range(4):
                last = nc.tensor.matmul(ps[:, b, :], ones[:], t3[:, 2 * b:2 * b + 2, :], start=True, stop=True)
            last.then_inc(att_p, 1)
            S.wait(att_d, 2)

            def scores(u):
                kind, s, t = units[u]
                b = 2 * (u % 2)
                if kind == "a":
                    r0 = 64 * (s % 2)
                    for g in range(3):
                        c = (g * 4 + s) // 2
                        last = nc.tensor.matmul(ps[:, b + g // 2, (g % 2) * L:(g % 2) * L + L],
                                                qk[r0:r0 + 64, c, t * P:t * P + P], qk[r0:r0 + 64, 6 + c, :],
                                                start=True, stop=True)
                else:
                    last = nc.tensor.matmul(ps[:, b, 0:L], qm[:, s, t * P:t * P + P], km[:, s, :],
                                            start=True, stop=True)
                last.then_inc(un_sc, 1)

            scores(0)
            for u, (kind, s, t) in enumerate(units):
                if u + 1 < len(units):
                    scores(u + 1)
                nb = 6 if kind == "a" else 2
                S.wait(un_pr)
                for j in range(nb):
                    last = nc.tensor.transpose(psf[:, 2048 + j * P:2048 + j * P + P], sc[:, u % 2, j * P:j * P + P],
                                               ident[:])
                last.then_inc(un_tp, 1)
                S.wait(un_pt)
                if u >= 2:
                    S.wait(un_out)
                for j in range(nb):
                    if kind == "a":
                        g, kt_ = divmod(j, 2)
                        hd = g * 4 + s
                        last = nc.tensor.matmul(ps[64 * (s % 2):64 * (s % 2) + 64, 6 + u % 2, 0:P],
                                                va[:, kt_, hd * 64:hd * 64 + 64], pt[:, u % 2, j * P:j * P + P],
                                                start=(j == 0), stop=(j == nb - 1))
                    else:
                        last = nc.tensor.matmul(ps[:, 6 + u % 2, 0:P], vm[:, j, s * P:s * P + P],
                                                pt[:, u % 2, j * P:j * P + P], start=(j == 0), stop=(j == nb - 1))
                last.then_inc(un_o, 1)
            S.wait(un_out, 2)
            S.wait(conv_done)
            for j in range(4):
                chans(lambda k: oa[:, k, :], 2, L)
            for j in range(4):
                chans(lambda k: zc[:, k, :], 6, L)
            for j in range(4):
                chans(lambda k: om[:, k, :], 4, L)
            all_drained()
            for j in range(4):
                chans(lambda k: mg[:, k, :], KD, L)
            norm(L)
            for t in range(2):
                for k in range(KD):
                    if t == 0:
                        S.wait(xh_done)
                    last = nc.tensor.matmul(ps[:, t, 0:36], h[:, k, t * P:t * P + P], rw[:, k, :],
                                            start=(k == 0), stop=(k == KD - 1))
            last.then_inc(rt_p, 1)
            for b in range(4):
                nc.tensor.matmul(ps[:, 4 + b, :], zero[:], x[:, 0, :], start=True, stop=False, skip_group_check=True)
            for g in range(16):
                S.wait(rt_dg)
                if g >= 4:
                    S.wait(rt_wb)
                nc.tensor.matmul(ps[:, g % 4, :], ones[:], dg[:, g % 2, :, :], start=True, stop=True).then_inc(rt_bc, 1)
            S.wait(rt_wb, 4)

            def gate_up(e):
                for half in range(2):
                    if e is not None:
                        pe.wait_ge(moe_gu, e(half))
                    for which in range(2):
                        n = slab.n
                        full = 16 * (n // SLOTS + 1)
                        s = n % SLOTS
                        pe.wait_ge(slot_full[s], full if slab.i is None
                                   else slab.i * (16 * slab.step // SLOTS) + full)
                        for c in range(2):
                            for k in range(KD):
                                last = nc.tensor.matmul(ps[:, 2 * half + which, c * L:c * L + L],
                                                        ring[:, s, k * 256 + c * P:k * 256 + c * P + P],
                                                        h[:, k, 0:L], start=(k == 0), stop=(k == KD - 1),
                                                        skip_group_check=True)
                        last.then_inc(slab_done, 1)
                        slab.n += 1

            def down(par, ready):
                pe.wait_ge(moe_gu, ready)
                for half in range(2):
                    n = slab.n
                    full = 16 * (n // SLOTS + 1)
                    s = n % SLOTS
                    pe.wait_ge(slot_full[s], full if slab.i is None else slab.i * (16 * slab.step // SLOTS) + full)
                    for c in range(4):
                        for k in range(4):
                            last = nc.tensor.matmul(
                                ps[:, 4 + 2 * half + c // 2, (c % 2) * L:(c % 2) * L + L],
                                ring[:, s, k * 512 + c * P:k * 512 + c * P + P], gu[:, par, k, :],
                                start=False, stop=False, skip_group_check=True)
                    last.then_inc(slab_done, 1)
                    slab.n += 1

            gate_up(None)
            with slabs((N_EXP - 2) // 2, 12) as i:
                for p in range(2):
                    gate_up(lambda half: i * 4 + (2 * p + half + 1))
                    down(p, i * 4 + (2 * p + 2))
            gate_up(lambda half: 2 * (N_EXP - 2) + half + 1)
            down(0, 2 * (N_EXP - 1))
            down(1, 2 * N_EXP)

        @block.tensor
        def _(pe):
            S = Side(pe)
            slab = Tally()

            def take():
                n = slab.n
                full = 16 * (n // SLOTS + 1)
                pe.wait_ge(slot_full[n % SLOTS], full if slab.i is None else slab.i * (16 * slab.step // SLOTS) + full)
                if n >= SLOTS:
                    pe.wait_ge(drained, slab.now(SLOTS - 1))
                slab.n += 1
                return n % SLOTS

            @contextmanager
            def slabs(trips, per):
                n0 = slab.n
                with pe.Fori(0, trips) as i:
                    slab.step, slab.i = per, i
                    yield i
                slab.n, slab.step, slab.i = n0 + per * trips, 0, None

            def all_drained():
                pe.wait_ge(drained, slab.now())

            def chans(rhs, kn, n, ready=None, k_ready=1):
                s = take()
                for c in range(2):
                    for k in range(kn):
                        if ready is not None and c == 0:
                            S.wait(ready, k_ready)
                        last = nc.tensor.matmul(ps[:, 2 * s + c, 0:n], ring[:, s, k * 256 + c * P:k * 256 + c * P + P],
                                                rhs(k), start=(k == 0), stop=(k == kn - 1))
                last.then_inc(slab_done, 1)

            def tokens(lhs, tiles):
                s = take()
                for t in range(tiles):
                    for k in range(KD):
                        last = nc.tensor.matmul(ps[:, 2 * s + t // 2, (t % 2) * 256:(t % 2) * 256 + 256],
                                                lhs(k, t), ring[:, s, k * 256:k * 256 + 256],
                                                start=(k == 0), stop=(k == KD - 1))
                last.then_inc(slab_done, 1)

            def norm(n):
                for k in range(KD):
                    S.wait(sq_done)
                    last = nc.tensor.matmul(ps[:, 7, 0:n], ones[:], h[:, k, 0:n], start=(k == 0), stop=(k == KD - 1))
                last.then_inc(ssq_done, 1)

            def ffn(n):
                for j in range(4):
                    chans(lambda k: h[:, k, 0:n], KD, n, h_done if j == 0 else None, n // L)
                with slabs(4, 4):
                    for j in range(4):
                        chans(lambda k: h[:, k, 0:n], KD, n)
                for j in range(2):
                    chans(lambda k: h[:, k, 0:n], KD, n)
                all_drained()
                with slabs(2, 8):
                    for pair in range(2):
                        k0 = 0
                        for kn in W2K:
                            s = take()
                            for k in range(kn):
                                for c in range(2):
                                    last = nc.tensor.matmul(
                                        ps[:, 2 * pair + c, 0:n], ring[:, s, k * 256 + c * P:k * 256 + c * P + P],
                                        hid[:, k0 + k, 0:n], start=(k0 + k == 0), stop=(k0 + k == KF - 1))
                            last.then_inc(slab_done, 1)
                            k0 += kn

            def gmlp(l):
                nt = 4 if l == 0 else 2
                S.wait(gm_v)
                for g in range(4):
                    for t in range(nt):
                        last = nc.tensor.matmul(ps[:, g, t * P:t * P + P], vg[:, t, g * P:g * P + P], ws[:, l, g, :],
                                                start=(t == 0), stop=(t == nt - 1), skip_group_check=True)
                    last.then_inc(gm_sv, 1)

            def gla(l, item0):
                nt = 4 if l == 0 else 2
                item = [item0, item0]
                S.wait(gm_out)

                def scores(e, d, hh, t):
                    b = item[0] % 2
                    cols = slice(t * P, t * P + P)
                    for lev in range(8):
                        lo, hi = (ex[:, e, lev, cols],) * 2 if lev < 7 else (kk[:, d, hh, cols], qq[:, hh, cols])
                        last = nc.tensor.matmul(ps[:, 2 * b + lev // 4, (lev % 4) * P:(lev % 4) * P + P],
                                                lo, hi, start=(lev % 4 == 0), stop=(lev % 4 == 3),
                                                skip_group_check=True)
                    last.then_inc(sc_done, 1)
                    item[0] += 1

                def values(hh, t):
                    S.wait(pm_done)
                    for lev in range(8):
                        last = nc.tensor.matmul(ps[:, 4 + hh % 2, t * P:t * P + P], vi[:, t, hh * P:hh * P + P],
                                                pm[:, item[1] % 2, lev, :], start=False, stop=False,
                                                skip_group_check=True)
                    last.then_inc(pv_done, 1)
                    item[1] += 1

                for hh in range(4):
                    if hh >= 2:
                        S.wait(o_out)
                    nc.tensor.matmul(ps[:, 4 + hh % 2, 0:nt * P], zero[:], x[:, 0, 0:nt * P],
                                     start=True, stop=False, skip_group_check=True)
                    for d in range(2):
                        e, order = d, seq[d]
                        S.wait(xq_done)
                        S.wait(xk_done)
                        for j in range(3):
                            last = nc.tensor.transpose(ps[:, 6, j * P:j * P + P],
                                                       ex[:, e, 8, order[j] * P:order[j] * P + P], ident[:])
                        last.then_inc(ktp_done, 1)
                        scores(e, d, hh, 0)
                        S.wait(kt_done)
                        for j in range(3):
                            last = nc.tensor.matmul(ps[:, 7, j * P:j * P + P], kt[:, j, :],
                                                    vi[:, order[j], hh * P:hh * P + P],
                                                    start=(j == 0), stop=(j == 2), skip_group_check=True)
                        last.then_inc(kv_done, 1)
                        for t in range(1, nt):
                            scores(e, d, hh, t)
                            values(hh, t - 1)
                        values(hh, nt - 1)
                        S.wait(st_done)
                        for j in range(1, 4):
                            t = order[j]
                            if t < nt:
                                last = nc.tensor.matmul(ps[:, 4 + hh % 2, t * P:t * P + P], st[:, j - 1, :],
                                                        ex[:, e, 7, t * P:t * P + P], start=False,
                                                        stop=(j == 3 and d == 1), skip_group_check=True)
                        last.then_inc(hd_done, 1)
                S.wait(o_out, 2)
                for hh in range(4):
                    S.wait(sq_done)
                    nc.tensor.matmul(ps[:, hh, 0:nt * P], ones[:], ex[:, 0, hh, 0:nt * P],
                                     start=True, stop=True).then_inc(ssq_done, 1)
                return item[0]

            S.wait(const_in, 16 * N_CONST)
            S.wait(zeroed)
            S.wait(silu_c)
            items = 0
            for l in range(DEPTH):
                n1 = T2 if l == 0 else L
                if l == 0:
                    for j in range(4):
                        chans(lambda k: cvec[:, k, :], KD, 2)
                with slabs(8 if l == 0 else 9, 4):
                    for j in range(4):
                        chans(lambda k: cvec[:, k, :], KD, 2)
                norm(T2)
                ffn(T2)
                norm(T2)
                for j in range(14):
                    if j in (4, 5):
                        tokens(lambda k, t: h[:, k, t * P:t * P + P], n1 // P)
                    elif j in (6, 7):
                        tokens(lambda k, t: h[:, k, t * P:t * P + P], 4)
                    else:
                        n = T2 if j < 4 else n1
                        chans(lambda k: h[:, k, 0:n], KD, n, h_done if j == 0 else None, 2)
                gmlp(l)
                items = gla(l, items)
                S.wait(bo_done)
                for j in range(4):
                    chans(lambda k: h[:, k, 0:n1], KD, n1)
                norm(n1)
                ffn(n1)
            second(pe, S, chans, tokens, all_drained, norm, slabs, take, slab)

        @block.scalar
        def _(act):
            S = Side(act)
            slab = Tally()

            def own(ins):
                ins.then_inc(act_own, 1)
                S.wait(act_own)

            def norm(src, n):
                act.wait_ge(drained, slab.now())
                for k in range(KD):
                    nc.scalar.activation(h[:, k, 0:n], src[:, k, 0:n], ACT.Square).then_inc(sq_done, 1)
                S.wait(inv_done)
                nc.scalar.activation(rs[:, 0:n], rs[:, 0:n], ACT.Sqrt).then_inc(rs_done, 1)

            def modulate(i, n):
                for k in range(KD):
                    S.wait(xh_done)
                    for s, cols in halves(n):
                        nc.scalar.activation(h[:, k, cols], h[:, k, cols], ACT.Identity,
                                             scale=gmod[:, i, k, s:s + 1],
                                             bias=mod[:, 3 * i * KD + k, s:s + 1]).then_inc(h_done, 1)

            def ffn(n):
                def pair(p):
                    s = slab.n % SLOTS
                    act.wait_ge(slab_done, slab.now(-1))
                    act.wait_ge(drained, slab.now(2))
                    nc.scalar.activation(sil[:, p, :, 0:n], ps[:, 2 * s:2 * s + 2, 0:n], ACT.Silu
                                         ).then_inc(silu_done, 1)
                    slab.n += 2
                n0 = slab.n
                with act.Fori(0, 5) as i:
                    slab.step, slab.i = 4, i
                    pair(0)
                    pair(1)
                slab.n, slab.step, slab.i = n0 + 20, 0, None
                pair(0)
                slab.n += 16

            def take(dst, src, func=ACT.Copy):
                act.wait_ge(slab_done, slab.now(-1))
                nc.scalar.activation(dst, src(slab.n % SLOTS), func).then_inc(drained, 1)
                slab.n += 1

            def log1p_exp_neg_abs(t):
                own(nc.scalar.activation(t, t, ACT.Abs))
                own(nc.scalar.activation(t, t, ACT.Exp, scale=-1.0))
                return nc.scalar.activation(t, t, ACT.Ln, bias=1.0)

            def gates(l):
                for d in range(2):
                    if d == 1:
                        S.wait(gate_d)
                    own(nc.scalar.activation(gt1, lf[:, d, :, :], ACT.Abs))
                    own(nc.scalar.activation(gt1, gt1, ACT.Exp, scale=-1.0))
                    nc.scalar.activation(gt1, gt1, ACT.Ln, bias=1.0).then_inc(gate_a, 1)
                    S.wait(gate_d)
                    nc.scalar.activation(kk[:, d, :, :], kk[:, d, :, :], ACT.Exp).then_inc(gate_a, 1)
                    if l == 1:
                        S.wait(gate_d)
                        log1p_exp_neg_abs(gt1).then_inc(gate_a, 1)

            def gla(l):
                nt = 4 if l == 0 else 2
                n = nt * P

                def decays(hd):
                    e = hd % 2
                    S.wait(dec_in)
                    if l == 0:
                        nc.scalar.activation(ex[:, e, :, :], ex[:, e, :, :], ACT.Exp)
                    else:
                        nc.scalar.activation(ex[:, e, 0:8, 0:n], ex[:, e, 0:8, 0:n], ACT.Exp)
                        nc.scalar.activation(ex[:, e, 8, :], ex[:, e, 8, :], ACT.Exp)
                    nc.scalar.activation(eb[:, e, :], be[:, e, :], ACT.Exp).then_inc(dec_out, 1)

                decays(0)
                for hd in range(8):
                    if hd + 1 < 8:
                        decays(hd + 1)
                    S.wait(ktp_done)
                    nc.scalar.activation(kt[:], ps[:, 6, 0:3 * P], ACT.Copy).then_inc(kt_done, 1)
                    S.wait(hd_done)
                    if hd % 2:
                        hh = hd // 2
                        nc.scalar.activation(h[:, 4 + hh, 0:n], ps[:, 4 + hh % 2, 0:n], ACT.Copy).then_inc(o_out, 1)
                S.wait(o_out, 4)
                for hh in range(4):
                    nc.scalar.activation(ex[:, 0, hh, 0:n], h[:, 4 + hh, 0:n], ACT.Square).then_inc(sq_done, 1)
                S.wait(inv_done)
                nc.scalar.activation(ex[:, 0, 4:8, 0:n], ex[:, 0, 4:8, 0:n], ACT.Sqrt).then_inc(rs_done, 1)

            act.dma_start(cvec[:], a["cvec"]).then_inc(const_in, 16)
            act.dma_start(vec[:], a["vec"]).then_inc(const_in, 16)
            act.dma_start(x[:, :, 0:L], a["xin"]).then_inc(const_in, 16)
            act.dma_start(x[:, :, L:T2], a["ctx"]).then_inc(const_in, 16)
            act.dma_start(shaped(work[:, 0:KD * L], KD, L), a["pos"]).then_inc(const_in, 16)
            for dst, name in ((ident, "ident"), (ones, "ones"), (keep, "keep"), (glamask, "glamask"), (ws, "ws"),
                              (blk64, "blk64"), (rot, "rot"), (amask, "amask"), (rw, "rw")):
                act.dma_start(dst[:], a[name]).then_inc(const_in, 16)
            act.dma_start(bs[:].rearrange("p l g t -> p (l g t)"), a["bs"].partition_broadcast(P)).then_inc(const_in, 16)
            act.dma_start(rb[:, 0:36], a["rb"].partition_broadcast(P)).then_inc(const_in, 16)
            act.dma_start(rb[:, 36:44], a["desc"].partition_broadcast(P)).then_inc(const_in, 16)
            act.dma_start(posi[:], a["positions"].partition_broadcast(P)).then_inc(const_in, 16)
            S.wait(const_in, 16 * N_CONST)
            nc.scalar.activation(cvec[:], cvec[:], ACT.Silu).then_inc(silu_c, 1)
            S.wait(start_d)
            own(nc.scalar.activation(lb1[:, 1], lb1[:, 0], ACT.Abs))
            own(nc.scalar.activation(lb1[:, 1], lb1[:, 1], ACT.Exp, scale=-1.0))
            nc.scalar.activation(lb1[:, 1], lb1[:, 1], ACT.Ln, bias=1.0).then_inc(start_a, 1)
            S.wait(start_d)
            nc.scalar.activation(cosn[:], cosn[:], ACT.Sin)
            nc.scalar.activation(sinn[:], sinn[:], ACT.Sin).then_inc(start_a, 1)
            for l in range(DEPTH):
                n1 = T2 if l == 0 else L
                slab.n += 36
                S.wait(mod_done)
                norm(x, T2)
                modulate(0, T2)
                ffn(T2)
                norm(x, T2)
                modulate(1, T2)
                for j in range(14):
                    if j < 4:
                        take(lf[:, j // 2, 2 * (j % 2):2 * (j % 2) + 2, :], lambda s: ps[:, 2 * s:2 * s + 2, :])
                        if j == 3:
                            S.wait(drained, 0)
                            act.wait_ge(drained, slab.now())
                            gates(l)
                    elif j < 8:
                        nt = 4 if j >= 6 else n1 // P
                        c = (j % 2) * 256
                        dst, func = (vg, ACT.Gelu_apprx_tanh) if j < 6 else (vi, ACT.Copy)
                        take(dst[:, 0:nt, c:c + 256],
                             lambda s: psf[:, s * 1024:s * 1024 + nt * 256].rearrange("p (t c) -> p t c", t=nt), func)
                    else:
                        dst, func = ((qq, ACT.Silu), (uu, ACT.Gelu_apprx_tanh), (og, ACT.Silu))[(j - 8) // 2]
                        c = 2 * (j % 2)
                        take(dst[:, c:c + 2, 0:n1], lambda s: ps[:, 2 * s:2 * s + 2, 0:n1], func)
                S.wait(gm_ms)
                nc.scalar.activation(vms[:], vms[:], ACT.Sqrt).then_inc(gm_rs, 1)
                gla(l)
                slab.n += 4
                norm(x, n1)
                modulate(2, n1)
                ffn(n1)
            norm(x, L)
            S.wait(xh_done, KD)
            S.wait(mem_in, 16)
            norm(memx, L)
            S.wait(xh_done, KD)
            for j in range(2):
                take(km[:, 2 * j:2 * j + 2, :], lambda s: ps[:, 2 * s:2 * s + 2, 0:L])
            for j in range(2):
                take(vm[:, :, j * 256:j * 256 + 256], lambda s: ps[:, 2 * s, :].rearrange("p (t c) -> p t c", t=2))
            norm(x, L)
            S.wait(xh_done, KD)
            cxf = cx.rearrange("p a b n -> p (a b) n")
            for j in range(20):
                if j < 9:
                    dst = cxf[:, 2 * j:2 * j + 2, :]
                elif j < 15:
                    dst = qk[:, 2 * (j - 9):2 * (j - 9) + 2, :]
                elif j < 18:
                    dst = va[:, :, (j - 15) * 256:(j - 15) * 256 + 256]
                else:
                    dst = qm[:, 2 * (j - 18):2 * (j - 18) + 2, :]
                if 15 <= j < 18:
                    take(dst, lambda s: ps[:, 2 * s, :].rearrange("p (t c) -> p t c", t=2))
                else:
                    take(dst, lambda s: ps[:, 2 * s:2 * s + 2, 0:L])
            n0 = slab.n
            with act.Fori(0, 3) as i:
                slab.step, slab.i = 4, i
                for j in range(4):
                    take(gt[:, bass.ds(i * 8 + 2 * j, 2), :], lambda s: ps[:, 2 * s:2 * s + 2, 0:L], ACT.Sigmoid)
            slab.n, slab.step, slab.i = n0 + 12, 0, None
            S.wait(conv_done)
            act.wait_ge(drained, slab.now())
            nc.scalar.activation(t3, qk, ACT.Square).then_inc(att_a, 1)
            S.wait(att_d)
            nc.scalar.activation(t4, t4, ACT.Sqrt).then_inc(att_a, 1)
            S.wait(att_d, 2)
            nc.scalar.activation(t3[:, 0:8, :], kqm, ACT.Square).then_inc(att_a, 1)
            S.wait(att_d)
            nc.scalar.activation(t4[:, 0:8, :], t4[:, 0:8, :], ACT.Sqrt).then_inc(att_a, 1)

            def exps(u):
                n = 3 * L if units[u][0] == "a" else L
                S.wait(un_mx)
                nc.scalar.activation(sc[:, u % 2, 0:n], sc[:, u % 2, 0:n], ACT.Exp, bias=vms[:, u % 2:u % 2 + 1],
                                     accum_out=vms[:, 2 + u % 2:3 + u % 2]).then_inc(un_ex, 1)

            exps(0)
            for u, (kind, s, t) in enumerate(units):
                if u + 1 < len(units):
                    exps(u + 1)
                n = 3 * L if kind == "a" else L
                S.wait(un_tp)
                nc.scalar.activation(pt[:, u % 2, 0:n], psf[:, 2048:2048 + n], ACT.Copy).then_inc(un_pt, 1)
                S.wait(un_o)
                if kind == "a":
                    r = slice(64 * (s % 2), 64 * (s % 2) + 64)
                    nc.scalar.activation(oa[r, s // 2, t * P:t * P + P], ps[r, 6 + u % 2, 0:P], ACT.Copy
                                         ).then_inc(un_out, 1)
                else:
                    nc.scalar.activation(om[:, s, t * P:t * P + P], ps[:, 6 + u % 2, 0:P], ACT.Copy
                                         ).then_inc(un_out, 1)
            slab.n += 16
            norm(x, L)
            S.wait(rt_d)
            nc.scalar.activation(ra[:, 1, :, 0:4], ra[:, 1, :, 0:4], ACT.Exp).then_inc(rt_a, 1)
            S.wait(rt_d)
            nc.scalar.activation(ra[:, 9, :, 0:1], ra[:, 9, :, 0:1], ACT.Exp).then_inc(rt_a, 1)
            for g in range(16):
                S.wait(rt_bc)
                nc.scalar.activation(wb[:, 2 * g:2 * g + 2, :], ps[:, g % 4, :], ACT.Copy).then_inc(rt_wb, 1)
            for half in range(2):
                act.wait_ge(slab_done, slab.n + 2 * half + 1)
                nc.scalar.activation(su[:, half, :, :], ps[:, 2 * half, :], ACT.Silu).then_inc(moe_s, 1)
            with act.Fori(0, N_EXP - 1) as i:
                for half in range(2):
                    act.wait_ge(slab_done, i * 6 + (slab.n + 4 + 2 * half + 1))
                    act.wait_ge(moe_gu, i * 2 + (half + 1))
                    nc.scalar.activation(su[:, half, :, :], ps[:, 2 * half, :], ACT.Silu).then_inc(moe_s, 1)
        @block.vector
        def _(dve):
            S = Side(dve)
            slab = Tally()

            def own(ins):
                ins.then_inc(dve_own, 1)
                S.wait(dve_own)

            def tt(o, i0, i1, op):
                return nc.vector.tensor_tensor(o, i0, i1, op)

            def ts(o, i0, s1, s2, op0, op1=ALU.bypass):
                return nc.vector.tensor_scalar(o, i0, s1, s2, op0, op1)

            def stt(o, i0, s, i1, op0, op1):
                return nc.vector.scalar_tensor_tensor(o, i0, s, i1, op0, op1)

            def inv_ms(n):
                S.wait(ssq_done)
                own(ts(rs[:, 0:n], ps[:, 7, 0:n], 1.0 / D, EPS, ALU.mult, ALU.add))
                nc.vector.reciprocal(rs[:, 0:n], rs[:, 0:n]).then_inc(inv_done, 1)

            def norm(n):
                inv_ms(n)
                S.wait(rs_done)
                for k in range(KD):
                    tt(h[:, k, 0:n], x[:, k, 0:n], rs[:, 0:n], ALU.mult).then_inc(xh_done, 1)

            def plain_norm(dst, src, g):
                inv_ms(L)
                S.wait(rs_done)
                for k in range(KD):
                    stt(dst[:, k, 0:L], src[:, k, 0:L], v(g, k), rs[:, 0:L], ALU.mult, ALU.mult).then_inc(xh_done, 1)

            def residual(chunks, pair, gate, n):
                for c in range(2):
                    for s, cols in halves(n):
                        last = stt(x[:, chunks[c], cols], ps[:, 2 * pair + c, cols], mod[:, gate[c], s:s + 1],
                                   x[:, chunks[c], cols], ALU.mult, ALU.add)
                return last

            def ffn(n, j):
                def pair(p, at):
                    s = slab.n % SLOTS + 1
                    S.wait(silu_done)
                    dve.wait_ge(slab_done, slab.now(-2))
                    tt(hid[:, at, 0:n], sil[:, p, :, 0:n], ps[:, 2 * s:2 * s + 2, 0:n], ALU.mult).then_inc(drained, 2)
                    slab.n += 2
                n0 = slab.n
                with S.loop(5, {silu_done: 2}) as i:
                    slab.step, slab.i = 4, i
                    pair(0, bass.ds(i * 4, 2))
                    pair(1, bass.ds(i * 4 + 2, 2))
                slab.n, slab.step, slab.i = n0 + 20, 0, None
                pair(0, slice(20, 22))
                for p in range(4):
                    dve.wait_ge(slab_done, slab.now(-4))
                    residual([2 * p, 2 * p + 1], p % 2, [j * KD + 2 * p, j * KD + 2 * p + 1], n).then_inc(drained, 4)
                    slab.n += 4

            def gates(l):
                for d in range(2):
                    f, k = lf[:, d, :, :], kk[:, d, :, :]
                    S.wait(gate_a)
                    own(stt(gt2, f, 0.0, gt1, ALU.min, ALU.subtract))
                    if l == 0:
                        tt(k, gt2, f, ALU.subtract).then_inc(gate_d, 1)
                        S.wait(gate_d)
                        own(nc.vector.tensor_copy(f, gt2))
                        S.wait(gate_a)
                    else:
                        for hh in range(4):
                            last = ts(gt2[:, hh, :], gt2[:, hh, :], lb1[:, 3, d, hh:hh + 1], None, ALU.add)
                        own(last)
                        tt(k, gt2, f, ALU.subtract).then_inc(gate_d, 1)
                        S.wait(gate_d)
                        for hh in range(4):
                            last = ts(gt1[:, hh, :], gt2[:, hh, :], lb1[:, 2, d, hh:hh + 1], None, ALU.subtract)
                        last.then_inc(gate_d, 1)
                        S.wait(gate_d)
                        for hh in range(4):
                            last = ts(f[:, hh, :], gt2[:, hh, :], lb1[:, 2, d, hh:hh + 1], None, ALU.max)
                        own(last)
                        S.wait(gate_a, 2)
                        own(tt(f, f, gt1, ALU.add))
                    if d == 0:
                        nc.vector.memset(be[:, 0, 0:1], 0.0).then_inc(gate_d, 1)
                        S.wait(gate_d)

            def gmlp(l):
                nt = 4 if l == 0 else 2
                dve.wait_ge(drained, slab.now())
                sq = ex[:, 1, 0:4, :]
                n = nt * 4
                own(tt(sq[:, 0:nt, :], vg[:, 0:nt, :], vg[:, 0:nt, :], ALU.mult))
                own(nc.vector.tensor_reduce(vms[:, 0:n], sq[:, 0:nt, :].rearrange("p t (g c) -> p (t g) c", g=4),
                                            AX, ALU.add))
                own(ts(vms[:, 0:n], vms[:, 0:n], 1.0 / P, EPS, ALU.mult, ALU.add))
                nc.vector.reciprocal(vms[:, 0:n], vms[:, 0:n]).then_inc(gm_ms, 1)
                S.wait(gm_rs)
                vv = vg[:, 0:nt, :].rearrange("p t (g c) -> p (t g) c", g=4)
                tt(vv, vv, vms[:, 0:n].unsqueeze(2).to_broadcast([P, n, P]), ALU.mult).then_inc(gm_v, 1)
                for g in range(4):
                    S.wait(gm_sv)
                    tl = ex[:, 1, g, 0:nt * P].rearrange("p (t c) -> p t c", t=nt)
                    own(stt(tl, ps[:, g, 0:nt * P].rearrange("p (t c) -> p t c", t=nt), v("g_gmlp", l * 4 + g),
                            bs[:, l, g, :].unsqueeze(1).to_broadcast([P, nt, P]), ALU.mult, ALU.add))
                    last = tt(h[:, g, 0:nt * P], ex[:, 1, g, 0:nt * P], uu[:, g, 0:nt * P], ALU.mult)
                last.then_inc(gm_out, 1)
                S.wait(gm_out)

            def gla(l, item0):
                nt = 4 if l == 0 else 2
                n = nt * P
                item = [item0]
                sub, add, mul = ALU.subtract, ALU.add, ALU.mult

                def decays(hd):
                    hh, d = divmod(hd, 2)
                    e = hd % 2
                    rev = slice(None, None, -1) if d else slice(None)
                    own(nc.vector.tensor_tensor_scan(bb[:, rev], keep[:], lf[:, d, hh, :][:, rev], 0.0, mul, add))
                    b64 = blocks(bb, 64)
                    early, late = early_late(b64, d)
                    ends = 63 * (1 - d)
                    ee, le = early[:, :, ends:ends + 1], late[:, :, ends:ends + 1]
                    if hd >= 2:
                        dve.wait_ge(hd_done, S.tally(hd_done).n + hd - 1)
                    own(tt(be[:, e, :], ee.squeeze(2), le.squeeze(2), add))
                    for lev in range(6):
                        m = 1 << lev
                        nb = n // (2 * m)
                        src_e, src_l = early_late(blocks(bb[:, 0:n], m), d)
                        dst_e, dst_l = early_late(blocks(ex[:, e, lev, 0:n], m), d)
                        at = (m - 1) * (1 - d)
                        ref = src_e[:, :, at:at + 1].to_broadcast([P, nb, m])
                        tt(dst_l, src_l, ref, sub)
                        tt(dst_e, ref, src_e, sub)
                    e6, l6 = early_late(blocks(ex[:, e, 6, 0:n], 64), d)
                    e7, l7 = early_late(blocks(ex[:, e, 7, 0:n], 64), d)
                    e8, l8 = early_late(blocks(ex[:, e, 8, :], 64), d)
                    eeb = ee.to_broadcast([P, 4, 64])
                    nc.vector.tensor_copy(l6, late[:, 0:nt])
                    tt(e6, eeb[:, 0:nt], early[:, 0:nt], sub)
                    nc.vector.tensor_copy(e7, early[:, 0:nt])
                    tt(l7, late[:, 0:nt], eeb[:, 0:nt], add)
                    tt(l8, le.to_broadcast([P, 4, 64]), late, sub)
                    tt(e8, be[:, e, :].unsqueeze(2).to_broadcast([P, 4, 64]), early, sub).then_inc(dec_in, 1)

                def times_q(hd):
                    hh, d = divmod(hd, 2)
                    e = hd % 2
                    S.wait(dec_out)
                    for lev in range(7):
                        m = 1 << lev
                        _, late = early_late(blocks(ex[:, e, lev, 0:n], m), d)
                        _, ql = early_late(blocks(qq[:, hh, 0:n], m), d)
                        tt(late, late, ql, mul)
                    tt(ex[:, e, 7, 0:n], ex[:, e, 7, 0:n], qq[:, hh, 0:n], mul).then_inc(xq_done, 1)

                def mask(hd):
                    S.wait(sc_done)
                    if item[0] >= 2:
                        dve.wait_ge(pv_done, item[0] - 1)
                    b = item[0] % 2
                    tt(pm[:, b, :, :], psf[:, b * 1024:b * 1024 + 1024].rearrange("p (v t) -> p v t", v=8),
                       gm[:, hd % 2, :, :], mul).then_inc(pm_done, 1)
                    item[0] += 1

                def states(hd):
                    e = hd % 2
                    order = seq[hd % 2]
                    S.wait(kv_done)
                    if hd >= 1:
                        dve.wait_ge(hd_done, S.tally(hd_done).n + hd)
                    own(nc.vector.tensor_copy(st[:, 0, :], ps[:, 7, 0:P]))
                    own(stt(st[:, 1, :], st[:, 0, :], eb[:, e, order[1]:order[1] + 1], ps[:, 7, P:2 * P], mul, add))
                    stt(st[:, 2, :], st[:, 1, :], eb[:, e, order[2]:order[2] + 1], ps[:, 7, 2 * P:3 * P], mul, add
                        ).then_inc(st_done, 1)

                decays(0)
                times_q(0)
                for hd in range(8):
                    if hd + 1 < 8:
                        decays(hd + 1)
                    mask(hd)
                    states(hd)
                    mask(hd)
                    if hd + 1 < 8:
                        times_q(hd + 1)
                    for t in range(2, nt):
                        mask(hd)
                S.count(hd_done, 8)
                S.wait(o_out, 4)
                S.wait(ssq_done, 4)
                r4 = ex[:, 0, 4:8, 0:n]
                own(ts(r4, ps[:, 0:4, 0:n], 1.0 / P, EPS, mul, add))
                nc.vector.reciprocal(r4, r4).then_inc(inv_done, 1)
                S.wait(rs_done)
                for hh in range(4):
                    own(stt(h[:, 4 + hh, 0:n], h[:, 4 + hh, 0:n], v("g_hgrn", l * 4 + hh), r4[:, hh, :], mul, mul))
                tt(h[:, 4:8, 0:n], h[:, 4:8, 0:n], og[:, :, 0:n], mul).then_inc(bo_done, 1)
                return item[0]

            nc.vector.memset(zero[:], 0.0).then_inc(zeroed, 1)
            nc.vector.memset(vms[:], 1.0)
            nc.vector.memset(work[:, WORK - 2 * T2:WORK], 0.0)
            S.wait(const_in, 16 * N_CONST)
            lb = v("lb", 0, 16).rearrange("p (d l c) -> p d l c", d=2, l=2)
            tt(lb1[:, 0], lb[:, :, 1, :], lb[:, :, 0, :], ALU.subtract).then_inc(start_d, 1)
            S.wait(start_d)
            S.wait(start_a)
            stt(lb1[:, 2], lb1[:, 0], 0.0, lb1[:, 1], ALU.min, ALU.subtract)
            own(ts(lb1[:, 3], lb1[:, 0], -1.0, 0.0, ALU.mult, ALU.min))
            own(tt(lb1[:, 3], lb1[:, 3], lb1[:, 1], ALU.subtract))
            ang, rnd = bb[:, 0:L], bb[:, L:T2]
            own(nc.vector.tensor_copy(ang, posi[:]))
            own(ts(ang, ang, v("inv"), None, ALU.mult))
            for dst, quarter in ((sinn, 0.0), (cosn, 0.25)):
                own(ts(rnd, ang, 1.0 / TWO_PI, quarter, ALU.mult, ALU.add))
                own(ts(rnd, rnd, ROUND, None, ALU.add))
                own(ts(rnd, rnd, ROUND, None, ALU.subtract))
                own(stt(dst[:], rnd, -PI_1, ang, ALU.mult, ALU.add))
                own(stt(dst[:], rnd, -PI_2, dst[:], ALU.mult, ALU.add))
                own(stt(dst[:], rnd, -PI_3, dst[:], ALU.mult, ALU.add))
                own(ts(dst[:], dst[:], quarter * TWO_PI, PI_MAX, ALU.add, ALU.min))
                own(ts(dst[:], dst[:], -PI_MAX, None, ALU.max))
            tt(x[:, :, 0:L], x[:, :, 0:L], shaped(work[:, 0:KD * L], KD, L), ALU.add).then_inc(start_d, 1)
            S.wait(start_d)
            S.wait(start_a)
            items = 0
            for l in range(DEPTH):
                n1 = T2 if l == 0 else L
                n0 = slab.n
                b0 = VEC["b_ada"][0] + l * N_MOD * KD
                with dve.Fori(0, 9) as i:
                    slab.step, slab.i = 4, i
                    for j in range(4):
                        dve.wait_ge(slab_done, slab.now(-1))
                        tt(mod[:, bass.ds(i * 8 + 2 * j, 2), :], ps[:, 2 * j:2 * j + 2, 0:2] if n0 % 4 == 0 else
                           ps[:, 2 * (slab.n % 4):2 * (slab.n % 4) + 2, 0:2],
                           vec[:, bass.ds(i * 8 + (b0 + 2 * j), 2)].unsqueeze(2).to_broadcast([P, 2, 2]), ALU.add
                           ).then_inc(drained, 1)
                        slab.n += 1
                slab.n, slab.step, slab.i = n0 + 36, 0, None
                dve.wait_ge(drained, slab.now())
                for i in range(3):
                    stt(gmod[:, i], mod[:, (3 * i + 1) * KD:(3 * i + 2) * KD, :], 1.0,
                        v("g_norm", (l * 3 + i) * KD, KD).unsqueeze(2).to_broadcast([P, KD, 2]), ALU.add, ALU.mult)
                for i in (2, 8):
                    g = mod[:, i * KD:(i + 1) * KD, :]
                    last = ts(g, g, 0.5, None, ALU.mult)
                last.then_inc(mod_done, 1)
                S.wait(mod_done)
                norm(T2)
                ffn(T2, 2)
                norm(T2)
                gates(l)
                slab.n += 14
                gmlp(l)
                items = gla(l, items)
                for j in range(4):
                    s = slab.n % SLOTS
                    dve.wait_ge(slab_done, slab.now(-1))
                    residual([2 * j, 2 * j + 1], s, [5 * KD + 2 * j, 5 * KD + 2 * j + 1], n1).then_inc(drained, 1)
                    slab.n += 1
                norm(n1)
                ffn(n1, 8)
            plain_norm(x, x, "g_final")
            S.wait(mem_in, 16)
            plain_norm(h, memx, "g_mem")
            slab.n += 4
            plain_norm(h, x, "g_mix")
            slab.n += 9
            dve.wait_ge(drained, slab.now())
            u, w = cx[:, 0], cx[:, 2]
            own(tt(u, w, u, ALU.mult))
            for c in range(6):
                own(ts(w[:, c, :], u[:, c, :], v("w_conv", 6 + c), None, ALU.mult))
                own(stt(w[:, c, 1:L], u[:, c, 0:L - 1], v("w_conv", c), w[:, c, 1:L], ALU.mult, ALU.add))
                own(stt(w[:, c, 0:L - 1], u[:, c, 1:L], v("w_conv", 12 + c), w[:, c, 0:L - 1], ALU.mult, ALU.add))
            tt(zc, w, cx[:, 1], ALU.mult).then_inc(conv_done, 1)
            S.wait(conv_done)
            slab.n += 23
            S.wait(att_p)
            own(ts(t4, psf[:, 0:AH * L].rearrange("p (c n) -> p c n", c=AH), 1.0 / 64, EPS, ALU.mult, ALU.add))
            nc.vector.reciprocal(t4, t4).then_inc(att_d, 1)
            S.wait(att_a, 2)
            stt(qk[:, 0:6, :], qk[:, 0:6, :], v("g_qa"), t4[:, 0:6, :], ALU.mult, ALU.mult)
            stt(qk[:, 6:12, :], qk[:, 6:12, :], v("g_ka"), t4[:, 6:12, :], ALU.mult, ALU.mult).then_inc(att_d, 1)
            S.wait(att_d, 2)
            S.wait(att_p)
            tt(t3, psf[:, 0:AH * L].rearrange("p (c n) -> p c n", c=AH),
               sinn[:].unsqueeze(1).to_broadcast([P, AH, L]), ALU.mult)
            own(tt(qk, qk, cosn[:].unsqueeze(1).to_broadcast([P, AH, L]), ALU.mult))
            tt(qk, qk, t3, ALU.add).then_inc(att_d, 1)
            S.wait(att_p)
            own(ts(t4[:, 0:8, :], psf[:, 0:8 * L].rearrange("p (c n) -> p c n", c=8), 1.0 / P, EPS,
                   ALU.mult, ALU.add))
            nc.vector.reciprocal(t4[:, 0:8, :], t4[:, 0:8, :]).then_inc(att_d, 1)
            S.wait(att_a, 2)
            stt(km, km, v("g_km"), t4[:, 0:4, :], ALU.mult, ALU.mult)
            stt(qm, qm, v("g_qm"), t4[:, 4:8, :], ALU.mult, ALU.mult).then_inc(att_d, 1)

            def scaled(u):
                kind, s, t = units[u]
                e = u % 2
                n = 3 * L if kind == "a" else L
                S.wait(un_sc)
                if u >= 2:
                    S.wait(un_tp)
                src = psf[:, e * 1024:e * 1024 + n]
                if kind == "a":
                    own(stt(sc[:, e, 0:n], src, 64 ** -0.5, amask[:, t, :], ALU.mult, ALU.add))
                else:
                    own(ts(sc[:, e, 0:n], src, P ** -0.5, None, ALU.mult))
                own(nc.vector.reduce_max(vms[:, 4 + e:5 + e], sc[:, e, 0:n], AX))
                ts(vms[:, e:e + 1], vms[:, 4 + e:5 + e], -1.0, None, ALU.mult).then_inc(un_mx, 1)

            scaled(0)
            for u, (kind, s, t) in enumerate(units):
                if u + 1 < len(units):
                    scaled(u + 1)
                e = u % 2
                n = 3 * L if kind == "a" else L
                S.wait(un_ex)
                own(nc.vector.reciprocal(vms[:, 6 + e:7 + e], vms[:, 2 + e:3 + e]))
                ts(sc[:, e, 0:n], sc[:, e, 0:n], vms[:, 6 + e:7 + e], None, ALU.mult).then_inc(un_pr, 1)
            for br in range(3):
                for j in range(4):
                    s = slab.n % SLOTS
                    dve.wait_ge(slab_done, slab.now(-1))
                    g = gt[:, br * KD + 2 * j:br * KD + 2 * j + 2, :]
                    m = mg[:, 2 * j:2 * j + 2, :]
                    if br == 0:
                        tt(m, g, ps[:, 2 * s:2 * s + 2, 0:L], ALU.mult).then_inc(drained, 1)
                    else:
                        dve.wait_ge(drained, slab.now(1))
                        tmp = t3[:, 2 * (j % 2):2 * (j % 2) + 2, :]
                        own(tt(tmp, g, ps[:, 2 * s:2 * s + 2, 0:L], ALU.mult))
                        tt(m, m, tmp, ALU.add).then_inc(drained, 1)
                    slab.n += 1
            for j in range(4):
                s = slab.n % SLOTS
                dve.wait_ge(slab_done, slab.now(-1))
                xc = x[:, 2 * j:2 * j + 2, 0:L]
                tt(xc, xc, ps[:, 2 * s:2 * s + 2, 0:L], ALU.add).then_inc(drained, 1)
                slab.n += 1
            plain_norm(h, x, "g_ffn")
            S.wait(rt_p)
            own(tt(lg[:], ps[:, 0:2, 0:36], rb[:, 0:36].unsqueeze(1).to_broadcast([P, 2, 36]), ALU.add))
            gl = lg[:, :, 0:4]
            el = lg[:, :, 4:36].rearrange("p t (g e) -> p t g e", g=4)

            def wide(col, n):
                return col.to_broadcast([P, 2, n])

            def one_hot(dst, src, top, n):
                own(nc.vector.tensor_reduce(top, src, AX, ALU.max))
                own(tt(dst, src, wide(top, n), ALU.is_equal))
                own(tt(dst, dst, rb[:, 36:36 + n].unsqueeze(1).to_broadcast([P, 2, n]), ALU.mult))
                own(nc.vector.tensor_reduce(ra[:, 10, :, 0:1], dst, AX, ALU.max))
                own(tt(dst, dst, wide(ra[:, 10, :, 0:1], n), ALU.is_equal))

            gm1, goh, tmp = ra[:, 0, :, 0:1], ra[:, 2, :, 0:4], ra[:, 3]
            one_hot(goh, gl, gm1, 4)
            tt(ra[:, 1, :, 0:4], gl, wide(gm1, 4), ALU.subtract).then_inc(rt_d, 1)
            S.wait(rt_d)
            sel = ra[:, 4]
            own(tt(sel, el[:, :, 0, :], wide(goh[:, :, 0:1], 8), ALU.mult))
            for g in range(1, 4):
                own(tt(tmp, el[:, :, g, :], wide(goh[:, :, g:g + 1], 8), ALU.mult))
                own(tt(sel, sel, tmp, ALU.add))
            m1, m2, o1, o2 = ra[:, 5, :, 0:1], ra[:, 6, :, 0:1], ra[:, 7], ra[:, 8]
            one_hot(o1, sel, m1, 8)
            own(stt(tmp, o1, -3e38, sel, ALU.mult, ALU.add))
            one_hot(o2, tmp, m2, 8)
            e2 = ra[:, 9, :, 0:1]
            tt(e2, m2, m1, ALU.subtract).then_inc(rt_d, 1)
            S.wait(rt_a, 2)
            z, w1, w2 = ra[:, 11, :, 0:1], ra[:, 11, :, 1:2], ra[:, 11, :, 2:3]
            own(nc.vector.tensor_reduce(z, ra[:, 1, :, 0:4], AX, ALU.add))
            own(stt(w1, e2, 1.0, z, ALU.add, ALU.mult))
            own(nc.vector.reciprocal(w1, w1))
            own(tt(w2, w1, e2, ALU.mult))
            own(tt(o1, o1, wide(w1, 8), ALU.mult))
            own(tt(o2, o2, wide(w2, 8), ALU.mult))
            own(tt(o1, o1, o2, ALU.add))
            for g in range(4):
                last = tt(rwt[:, :, g * 8:g * 8 + 8], o1, wide(goh[:, :, g:g + 1], 8), ALU.mult)
            own(last)
            for g in range(16):
                if g >= 2:
                    S.wait(rt_bc)
                for j in range(4):
                    e, t = 2 * g + j // 2, j % 2
                    last = ts(dg[:, g % 2, j, :], ident[:], rwt[:, t, e:e + 1], None, ALU.mult)
                last.then_inc(rt_dg, 1)
            S.wait(rt_wb, 16)

            def hidden(par, e, half, s_ready, slabs_ready):
                dve.wait_ge(moe_s, s_ready)
                own2(tt(tt2[:, half, :, :], su[:, half, :, :], wb[:, e, :].to_broadcast([P, 2, L]), ALU.mult))
                dve.wait_ge(slab_done, slabs_ready)
                tt(gu[:, par, 2 * half:2 * half + 2, :], tt2[:, half, :, :],
                   ps[:, 2 * half + 1, :].rearrange("p (c n) -> p c n", c=2), ALU.mult).then_inc(moe_gu, 1)

            def own2(ins):
                own(ins)

            for half in range(2):
                hidden(0, slice(0, 1), half, half + 1, slab.n + 2 * half + 2)
            own_steps = {dve_own: 4}
            with S.loop((N_EXP - 2) // 2, own_steps) as i:
                for p in range(2):
                    for half in range(2):
                        hidden(1 - p, bass.ds(i * 2 + (1 + p), 1), half, i * 4 + (2 + 2 * p + half + 1),
                               i * 12 + (slab.n + 4 + 6 * p + 2 * half + 2))
            for half in range(2):
                hidden(1, slice(N_EXP - 1, N_EXP), half, 2 * (N_EXP - 1) + half + 1,
                       slab.n + 4 + 6 * (N_EXP - 2) + 2 * half + 2)
            slab.n += 6 * N_EXP
            dve.wait_ge(slab_done, slab.now())
            tt(x[:, :, 0:L], x[:, :, 0:L], psf[:, 2048:4096].rearrange("p (c n) -> p c n", c=KD), ALU.add
               ).then_inc(fin, 1)
        @block.gpsimd
        def _(pool):
            S = Side(pool)
            for l in range(DEPTH):
                n = T2 if l == 0 else L
                for hd in range(8):
                    hh, d = divmod(hd, 2)
                    e = hd % 2
                    S.wait(dec_out)
                    for lev in range(7):
                        m = 1 << lev
                        early, _ = early_late(blocks(ex[:, e, lev, 0:n], m), d)
                        ke, _ = early_late(blocks(kk[:, d, hh, 0:n], m), d)
                        nc.gpsimd.tensor_tensor(early, early, ke, ALU.mult)
                    nc.gpsimd.tensor_tensor(ex[:, e, 8, :], ex[:, e, 8, :], kk[:, d, hh, :], ALU.mult
                                            ).then_inc(xk_done, 1)
_OUT = (P, KD, L)


def slabs_of(w, cols=256):
    k, n = w.shape
    return w.reshape(k // P, P, n // cols, cols).transpose(2, 1, 0, 3).reshape(n // cols, P, -1)


def chans_of(w):
    return w.reshape(-1, P).T


def constants():
    f = np.float32
    rows = np.repeat(np.arange(L // 64), 64).astype(f)
    cols = np.tile(np.arange(64), L // 64).astype(f)
    freq = (f(10000.0) ** (-np.arange(256, dtype=f) / f(256))).astype(f)
    emb = []
    for p in (rows, cols):
        ang = p[:, None] * freq[None, :]
        emb += [np.sin(ang), np.cos(ang)]
    pos = np.concatenate(emb, axis=-1).astype(f)
    c = {"pos": np.ascontiguousarray(pos.T.reshape(KD, P, L).transpose(1, 0, 2))}
    c["ident"] = np.eye(P, dtype=f)
    c["ones"] = np.ones((P, P), f)
    c["keep"] = np.ascontiguousarray(np.broadcast_to((np.arange(T2) % 64 != 0).astype(f), (P, T2)))
    s, t = np.arange(P)[:, None], np.arange(P)[None, :]
    m = np.zeros((P, 2, 8, P), f)
    for lev in range(LEVELS):
        size = 1 << lev
        same = (s // (2 * size)) == (t // (2 * size))
        m[:, 0, lev] = same & (s // size % 2 == 0) & (t // size % 2 == 1)
        m[:, 1, lev] = same & (s // size % 2 == 1) & (t // size % 2 == 0)
    m[:, :, 7] = (s == t)[:, None, :]
    c["glamask"] = m.reshape(P, -1)
    c["blk64"] = (s // 64 == t // 64).astype(f)
    r = np.zeros((P, P), f)
    for b in (0, 64):
        for i in range(8):
            r[b + 8 + i, b + i] = -1
            r[b + i, b + 8 + i] = 1
    c["rot"] = r
    i, j = np.arange(L)[:, None], np.arange(L)[None, :]
    masks = []
    for window, dil in ((128, 1), (512, 4), (2048, 16)):
        ok = (i % dil == j % dil) & (np.abs(i - j) // dil <= window // (2 * dil))
        masks.append(np.where(ok, f(0), f(NEG)))
    c["amask"] = np.ascontiguousarray(np.concatenate(masks, 1).astype(f).reshape(2, P, 3 * L).transpose(1, 0, 2))
    c["desc"] = np.arange(8, 0, -1).astype(f)
    return c


def layout(inp):
    a = dict(constants())
    A = {k: np.asarray(val) for k, val in inp.items()}
    cat = np.concatenate
    a["cvec"] = np.stack([A["c"][0], A["c_ctx"]], -1).reshape(KD, P, 2).transpose(1, 0, 2)
    for name, src in (("xin", A["x"][0]), ("ctx", A["ctx"][0]), ("memx", A["mem_2"][0])):
        a[name] = src.T.reshape(KD, P, L).transpose(1, 0, 2)
    inv = np.zeros((P, 1), np.float32)
    f = (np.float32(500000.0) ** (-np.arange(0, 16, 2, dtype=np.float32) / np.float32(16))).astype(np.float32)
    for b in (0, 8, 64, 72):
        inv[b:b + 8, 0] = f
    two = lambda g: np.tile(g.reshape(-1), 2).reshape(P, 1)
    cols = {
        "b_ada": chans_of(A["b_ada"]),
        "g_norm": cat([chans_of(A[n][l]) for l in range(DEPTH) for n in ("norm_ffn1_g", "norm_mix_g", "norm_ffn2_g")], 1),
        "g_gmlp": chans_of(A["gmlp_norm_g"]),
        "lb": cat([chans_of(A["hgrn_lb_fwd"]), chans_of(A["hgrn_lb_bwd"])], 1),
        "g_hgrn": chans_of(A["hgrn_norm_g"]), "g_final": chans_of(A["norm_final_g"]),
        "g_mix": chans_of(A["g_mix_2"]), "g_mem": chans_of(A["g_mem_2"]),
        "g_qa": two(A["g_qn_attn_2"]), "g_ka": two(A["g_kn_attn_2"]),
        "w_conv": chans_of(A["w_conv_2"]), "g_qm": A["g_qn_mem_2"].reshape(P, 1), "g_km": A["g_kn_mem_2"].reshape(P, 1),
        "g_ffn": chans_of(A["g_ffn_2"]), "inv": inv}
    a["vec"] = cat([cols[n] for n in VEC], 1)
    a["ws"] = A["gmlp_ws"].transpose(3, 0, 1, 2)
    a["bs"] = A["gmlp_bs"].reshape(-1)
    a["rb"] = cat([A["b_router_group_2"].reshape(-1), A["b_router_expert_2"].reshape(-1)])
    a["rw"] = cat([A["w_router_group_2"][0], A["w_router_expert_2"][0]], 1).reshape(KD, P, 36).transpose(1, 0, 2)
    a["positions"] = A["positions_2"].reshape(-1)
    a["w_ada"] = cat([slabs_of(A["w_ada"][l]) for l in range(DEPTH)])
    a["w13"] = cat([np.stack([slabs_of(A[f"ffn{i}_w1"][l]), slabs_of(A[f"ffn{i}_w3"][l])], 1).reshape(22, P, SLAB)
                    for l in range(DEPTH) for i in (1, 2)])
    a["w2"] = cat([slabs_of(A[f"ffn{i}_w2"][l]) for l in range(DEPTH) for i in (1, 2)])
    order = [6, 7, 8, 9, 2, 3, 10, 11, 4, 5, 0, 1, 12, 13]
    a["w_in"] = cat([slabs_of(A["w_in"][l])[order] for l in range(DEPTH)])
    a["w_out"] = cat([slabs_of(A["w_out"][l]) for l in range(DEPTH)])
    a["w_mem"] = slabs_of(A["w_mem_kv_2"][0])
    order = list(range(9, 18)) + list(range(0, 9)) + list(range(18, 32))
    a["w_in2"] = slabs_of(A["w_in_2"][0])[order]
    a["w_pa"], a["w_pc"], a["w_pm"], a["w_out2"] = (slabs_of(A[n][0]) for n in (
        "w_proj_attn_2", "w_proj_conv_2", "w_proj_mem_2", "w_out_2"))
    gu, dn = [], []
    for e in range(N_EXP):
        g, u = slabs_of(A["w_gate_2"][0, e]), slabs_of(A["w_up_2"][0, e])
        gu.append([g[0], u[0], g[1], u[1]])
        dn.append(list(slabs_of(A["w_down_2"][0, e], 512)))
    moe = list(gu[0])
    for e in range(1, N_EXP):
        moe += gu[e] + dn[e - 1]
    a["w_moe"] = np.stack(moe + dn[-1])
    return {k: np.ascontiguousarray(val) for k, val in a.items()}


def kernel(**inputs):
    import concourse.bacc as bacc
    from concourse.bass_utils import run_bass_kernel_spmd

    nc = bacc.Bacc("TRN2", target_bir_lowering=False, num_devices=1)
    arrays = layout(inputs)
    aps = {n: nc.dram_tensor(f"in_{n}", arr.shape, mybir.dt.from_np(arr.dtype), kind="ExternalInput").ap()
           for n, arr in arrays.items()}
    out = nc.dram_tensor("result", _OUT, F32, kind="ExternalOutput").ap()
    build(nc, aps, out)
    r = run_bass_kernel_spmd(nc, [{f"in_{n}": arr for n, arr in arrays.items()}], core_ids=[0])
    got = r.results[0]["result"]
    return np.ascontiguousarray(got.transpose(1, 0, 2).reshape(D, L).T).reshape(1, L, D)
```

```python
from contextlib import ExitStack, contextmanager

import numpy as np
import concourse.bass as bass
from concourse import mybir

F32 = mybir.dt.float32
I32 = mybir.dt.int32
ALU = mybir.AluOpType
ACT = mybir.ActivationFunctionType
AX = mybir.AxisListType.X

P = 128
D = 1024
KD = D // P
L = 256
T2 = 2 * L
FF = 2816
KF = FF // P
DEPTH = 2
N_MOD = 9
HEADS = 4
EPS = 1e-6
SLOTS = 4
SLAB = KD * 256
W2K = (6, 6, 5, 5)
LEVELS = 7
N_EXP = 32
EXP_FF = 512
AH = 12
CONV_W = 768
NEG = -1e30
WORK = 24064
TWO_PI = 6.283185307179586
PI_1 = 6.28125
PI_2 = 0.0019350051879882812
PI_3 = TWO_PI - PI_1 - PI_2
PI_MAX = 3.1415925
ROUND = 12582912.0
CAP = 64
EH = EXP_FF // P

VEC = {}
_n = 0
for _name, _w in (("b_ada", DEPTH * N_MOD * KD), ("g_norm", DEPTH * 3 * KD), ("g_gmlp", DEPTH * 4), ("lb", 2 * DEPTH * 4),
                  ("g_hgrn", DEPTH * 4), ("g_final", KD), ("g_mix", KD), ("g_mem", KD), ("g_qa", 1), ("g_ka", 1),
                  ("w_conv", 3 * 6), ("g_qm", 1), ("g_km", 1), ("g_ffn", KD), ("inv", 1), ("slot", 1)):
    VEC[_name] = (_n, _n + _w)
    _n += _w
N_VEC = _n


class Tally:

    def __init__(self):
        self.n, self.step, self.i = 0, 0, None

    def now(self, back=0):
        return self.n - back if self.i is None else self.i * self.step + (self.n - back)


class Side:

    def __init__(self, eng):
        self.eng, self.seen = eng, {}

    def tally(self, sem):
        if sem not in self.seen:
            self.seen[sem] = Tally()
        return self.seen[sem]

    def count(self, sem, k=1):
        self.tally(sem).n += k

    def next(self, sem, k=1):
        self.count(sem, k)
        return self.tally(sem).now()

    @contextmanager
    def loop(self, trips, steps):
        before = {}
        with self.eng.Fori(0, trips) as i:
            for sem, k in steps.items():
                t = self.tally(sem)
                before[sem] = t.n
                t.step, t.i = k, i
            yield i
        for sem, k in steps.items():
            t = self.seen[sem]
            assert t.n == before[sem] + k, (sem, t.n - before[sem], k)
            t.n, t.step, t.i = before[sem] + k * trips, 0, None


def build(nc, a, out):
    with ExitStack() as ctx:
        def sb(name, shape, dt=F32):
            return ctx.enter_context(nc.sbuf_tensor(name, shape, dt))

        def sem(name):
            return ctx.enter_context(nc.semaphore(name))

        x = sb("x", [P, KD, T2])
        h = sb("h", [P, KD, T2])
        ring = sb("ring", [P, SLOTS, SLAB])
        rs = sb("rs", [P, T2])
        vec = sb("vec", [P, N_VEC])
        ident = sb("ident", [P, P])
        ones = sb("ones", [P, P])
        zero = sb("zero", [P, P])
        cvec = sb("cvec", [P, KD, 2])
        mod = sb("mod", [P, N_MOD * KD, 2])
        gmod = sb("gmod", [P, 3, KD, 2])
        glamask = sb("glamask", [P, 2 * 8 * P])
        pmt = sb("pmt", [P, 2 * 8 * P])
        kt = sb("kt", [P, 3, P])
        st = sb("st", [P, 3, P])
        keep = sb("keep", [P, T2])
        ws = sb("ws", [P, DEPTH, 4, P])
        bs = sb("bs", [P, DEPTH, 4, P])
        be = sb("be", [P, 2, 4])
        eb = sb("eb", [P, 2, 4])
        lb1 = sb("lb1", [P, 4, 2, 4])
        vms = sb("vms", [P, 16])
        blk64 = sb("blk64", [P, P])
        rot = sb("rot", [P, P])
        amask = sb("amask", [P, 2, 3 * L])
        rw = sb("rw", [P, KD, 36])
        rb = sb("rb", [P, 36 + 8])
        posi = sb("posi", [P, L], I32)
        cosn = sb("cosn", [P, L])
        sinn = sb("sinn", [P, L])
        work = sb("work", [P, WORK])
        ps = ctx.enter_context(nc.psum_tensor("ps", [P, 8, 512], F32))
        psf = ps[:].rearrange("p b n -> p (b n)")

        off = [0]

        def shaped(v, *shape):
            names = "abcd"[:len(shape)]
            return v if len(shape) == 1 else v.rearrange(
                f"p ({' '.join(names)}) -> p {' '.join(names)}", **dict(zip(names, shape)))

        def part(*shape):
            n = int(np.prod(shape))
            off[0] += n
            assert off[0] <= WORK, off[0]
            return shaped(work[:, off[0] - n:off[0]], *shape)

        hid = part(KF, T2)
        sil = part(2, 2, T2)
        mrow = work[0:2, 20480:21504]
        off[0] = 0
        lf = part(2, 4, T2)
        kk = part(2, 4, T2)
        vi = part(4, 512)
        qq = part(4, T2)
        og = part(4, T2)
        ex = part(2, LEVELS + 2, T2)
        bb = part(T2)
        gt1, uu = ex[:, 0, 0:4, :], ex[:, 0, 4:8, :]
        gt2, vg = ex[:, 1, 0:4, :], ex[:, 1, 4:8, :]
        off[0] = 0
        qk = part(AH, L)
        km = part(4, L)
        qm = part(4, L)
        kqm = shaped(work[:, 12 * L:20 * L], 8, L)
        va = part(2, 768)
        vm = part(2, 512)
        at = off[0]
        cx = part(3, 6, L)
        mg = part(KD, L)
        t3 = shaped(work[:, at:at + AH * L], AH, L)
        t4 = shaped(work[:, at + AH * L:at + 2 * AH * L], AH, L)
        gt = part(24, L)
        oa = part(2, L)
        zc = part(6, L)
        om = part(4, L)
        memx = gt[:, 0:KD, :]
        off[0] = 0
        wb = part(N_EXP, L)
        gu = part(2, 4, L)
        su = part(2, 2, L)
        tt2 = part(2, 2, L)
        lg = part(2, 36)
        ra = part(12, 2, 8)
        rwt = part(2, 32)
        used = part(2, 32)
        top = part(1)
        count = part(1).bitcast(I32)
        ht = part(2, D)
        hg = part(KD, P)
        taken = part(1, L)
        rank = part(1, L)
        pick_s = part(1, L)
        pick_w = part(1, L)
        pick_t = part(2, P)
        sg = part(EH, CAP)
        hv = part(2, EH, CAP)
        yt = part(D)
        pm = shaped(pmt[:], 2, 8, P)
        gm = shaped(glamask[:], 2, 8, P)
        sc = shaped(pmt[:, 0:2 * 3 * L], 2, 3 * L)
        pt = shaped(glamask[:, 0:2 * 3 * L], 2, 3 * L)
        dg = shaped(pmt[:, 0:1024], 2, 4, P)

        slot_full = [sem(f"slot_full{i}") for i in range(SLOTS)]
        const_in = sem("const_in")
        mem_in = sem("mem_in")
        out_in = sem("out_in")
        slab_done = sem("slab_done")
        drained = sem("drained")
        silu_c = sem("silu_c")
        start_d = sem("start_d")
        start_a = sem("start_a")
        zeroed = sem("zeroed")
        silu_done = sem("silu_done")
        mod_done = sem("mod_done")
        sq_done = sem("sq_done")
        ssq_done = sem("ssq_done")
        inv_done = sem("inv_done")
        rs_done = sem("rs_done")
        xh_done = sem("xh_done")
        h_done = sem("h_done")
        act_own = sem("act_own")
        dve_own = sem("dve_own")
        gate_a = sem("gate_a")
        gate_d = sem("gate_d")
        gm_ms = sem("gm_ms")
        gm_rs = sem("gm_rs")
        gm_v = sem("gm_v")
        gm_sv = sem("gm_sv")
        gm_out = sem("gm_out")
        dec_in = sem("dec_in")
        dec_out = sem("dec_out")
        xq_done = sem("xq_done")
        xk_done = sem("xk_done")
        ktp_done = sem("ktp_done")
        kt_done = sem("kt_done")
        kv_done = sem("kv_done")
        st_done = sem("st_done")
        sc_done = sem("sc_done")
        pm_done = sem("pm_done")
        pv_done = sem("pv_done")
        hd_done = sem("hd_done")
        o_out = sem("o_out")
        bo_done = sem("bo_done")
        conv_done = sem("conv_done")
        att_a = sem("att_a")
        att_d = sem("att_d")
        att_p = sem("att_p")
        un_sc = sem("un_sc")
        un_mx = sem("un_mx")
        un_ex = sem("un_ex")
        un_pr = sem("un_pr")
        un_tp = sem("un_tp")
        un_pt = sem("un_pt")
        un_o = sem("un_o")
        un_out = sem("un_out")
        rt_p = sem("rt_p")
        rt_d = sem("rt_d")
        rt_a = sem("rt_a")
        rt_dg = sem("rt_dg")
        rt_bc = sem("rt_bc")
        rt_wb = sem("rt_wb")
        moe_s = sem("moe_s")
        moe_gu = sem("moe_gu")
        rt_used = sem("rt_used")
        rt_cnt = sem("rt_cnt")
        rt_max = sem("rt_max")
        mrow_out = sem("mrow_out")
        mrow_turned = sem("mrow_turned")
        ht_tp = sem("ht_tp")
        ht_out = sem("ht_out")
        pick_done = sem("pick_done")
        pick_tp = sem("pick_tp")
        pick_out = sem("pick_out")
        pick_wd = sem("pick_wd")
        hg_pe = sem("hg_pe")
        hg_a = sem("hg_a")
        hg_d = sem("hg_d")
        sg_done = sem("sg_done")
        hv_done = sem("hv_done")
        yt_a = sem("yt_a")
        yt_d = sem("yt_d")
        spread = sem("spread")
        fin = sem("fin")
        N_CONST = 18

        def v(name, i0=0, n=1):
            c = VEC[name][0] + i0
            return vec[:, c:c + n]

        def halves(n):
            return [(0, slice(0, L)), (1, slice(L, T2))][:n // L]

        def early_late(view, d):
            return view[:, :, d, :], view[:, :, 1 - d, :]

        def blocks(view, m):
            return view.rearrange("p (n two m) -> p n two m", two=2, m=m)

        seq = ([2, 3, 0, 1], [3, 2, 1, 0])
        units = [("a", s, t) for s in range(4) for t in range(2)] + [("m", s, t) for s in range(4) for t in range(2)]

        block = ctx.enter_context(nc.Block())

        @block.sync
        def _(sp):
            S = Side(sp)
            sent = Tally()

            def send(src, width):
                n = sent.n
                if n >= SLOTS:
                    sp.wait_ge(slab_done, sent.now(SLOTS - 1))
                sp.dma_start(ring[:, n % SLOTS, 0:width], src).then_inc(slot_full[n % SLOTS], 16)
                sent.n += 1

            def stream(arr, first, count, width=SLAB):
                trips, rest = divmod(count, SLOTS)
                if sent.n == 0:
                    for j in range(SLOTS):
                        send(arr[first + j], width)
                    first, trips = first + SLOTS, trips - 1
                if trips > 1:
                    n0 = sent.n
                    with sp.Fori(0, trips) as i:
                        sent.step, sent.i = SLOTS, i
                        for j in range(SLOTS):
                            send(arr[i * SLOTS + (first + j)], width)
                    sent.n, sent.step, sent.i = n0 + trips * SLOTS, 0, None
                    first += trips * SLOTS
                    trips = 0
                for j in range(trips * SLOTS + rest):
                    send(arr[first + j], width)

            def ffn(f):
                stream(a["w13"], f * 22, 22)
                for pair in range(4):
                    k0 = 0
                    for k in W2K:
                        send(a["w2"][f * 4 + pair, :, k0 * 256:(k0 + k) * 256], k * 256)
                        k0 += k

            for l in range(DEPTH):
                stream(a["w_ada"], l * 36, 36)
                ffn(2 * l)
                stream(a["w_in"], l * 14, 14)
                stream(a["w_out"], l * 4, 4)
                ffn(2 * l + 1)
            sp.wait_ge(slab_done, sent.now())
            sp.dma_start(memx, a["memx"]).then_inc(mem_in, 16)
            stream(a["w_mem"], 0, 4)
            stream(a["w_in2"], 0, 32)
            stream(a["w_pa"], 0, 4, 2 * 256)
            stream(a["w_pc"], 0, 4, 6 * 256)
            stream(a["w_pm"], 0, 4, 4 * 256)
            stream(a["w_out2"], 0, 4)
            stream(a["w_moe"], 0, 6 * N_EXP)
            sp.wait_ge(fin, S.next(fin))
            n = 1
            sp.dma_start(out, x[:, :, 0:L]).then_inc(out_in, 16)
            sp.wait_ge(out_in, 16 * n)

        def second(pe, S, chans, tokens, all_drained, norm, slabs, landed, slab):
            norm(L)
            S.count(xh_done, 7 * KD)
            norm(L)
            for j in range(2):
                chans(lambda k: h[:, k, 0:L], KD, L, xh_done if j == 0 else None)
            for j in range(2):
                tokens(lambda k, t: h[:, k, t * P:t * P + P], 2)
            norm(L)
            for j in range(20):
                if 15 <= j < 18:
                    tokens(lambda k, t: h[:, k, t * P:t * P + P], 2)
                else:
                    chans(lambda k: h[:, k, 0:L], KD, L, xh_done if j == 0 else None)
            with slabs(3, 4):
                for j in range(4):
                    chans(lambda k: h[:, k, 0:L], KD, L)
            all_drained()
            pe.wait_ge(att_a, S.next(att_a))
            for b in range(6):
                last = nc.tensor.matmul(ps[:, b, :], blk64[:], t3[:, 2 * b:2 * b + 2, :], start=True, stop=True)
            last.then_inc(att_p, 1)
            pe.wait_ge(att_d, S.next(att_d, 2))
            for b in range(6):
                last = nc.tensor.matmul(ps[:, b, :], rot[:], qk[:, 2 * b:2 * b + 2, :], start=True, stop=True)
            last.then_inc(att_p, 1)
            pe.wait_ge(att_d, S.next(att_d))
            pe.wait_ge(att_a, S.next(att_a, 2))
            for b in range(4):
                last = nc.tensor.matmul(ps[:, b, :], ones[:], t3[:, 2 * b:2 * b + 2, :], start=True, stop=True)
            last.then_inc(att_p, 1)
            pe.wait_ge(att_d, S.next(att_d, 2))

            def scores(u):
                kind, s, t = units[u]
                b = 2 * (u % 2)
                if kind == "a":
                    r0 = 64 * (s % 2)
                    for g in range(3):
                        c = (g * 4 + s) // 2
                        last = nc.tensor.matmul(ps[:, b + g // 2, (g % 2) * L:(g % 2) * L + L],
                                                qk[r0:r0 + 64, c, t * P:t * P + P], qk[r0:r0 + 64, 6 + c, :],
                                                start=True, stop=True)
                else:
                    last = nc.tensor.matmul(ps[:, b, 0:L], qm[:, s, t * P:t * P + P], km[:, s, :],
                                            start=True, stop=True)
                last.then_inc(un_sc, 1)

            scores(0)
            for u, (kind, s, t) in enumerate(units):
                if u + 1 < len(units):
                    scores(u + 1)
                nb = 6 if kind == "a" else 2
                pe.wait_ge(un_pr, S.next(un_pr))
                for j in range(nb):
                    last = nc.tensor.transpose(psf[:, 2048 + j * P:2048 + j * P + P], sc[:, u % 2, j * P:j * P + P],
                                               ident[:])
                last.then_inc(un_tp, 1)
                pe.wait_ge(un_pt, S.next(un_pt))
                if u >= 2:
                    pe.wait_ge(un_out, S.next(un_out))
                for j in range(nb):
                    if kind == "a":
                        g, kt_ = divmod(j, 2)
                        hd = g * 4 + s
                        last = nc.tensor.matmul(ps[64 * (s % 2):64 * (s % 2) + 64, 6 + u % 2, 0:P],
                                                va[:, kt_, hd * 64:hd * 64 + 64], pt[:, u % 2, j * P:j * P + P],
                                                start=(j == 0), stop=(j == nb - 1))
                    else:
                        last = nc.tensor.matmul(ps[:, 6 + u % 2, 0:P], vm[:, j, s * P:s * P + P],
                                                pt[:, u % 2, j * P:j * P + P], start=(j == 0), stop=(j == nb - 1))
                last.then_inc(un_o, 1)
            pe.wait_ge(un_out, S.next(un_out, 2))
            pe.wait_ge(conv_done, S.next(conv_done))
            for j in range(4):
                chans(lambda k: oa[:, k, :], 2, L)
            for j in range(4):
                chans(lambda k: zc[:, k, :], 6, L)
            for j in range(4):
                chans(lambda k: om[:, k, :], 4, L)
            all_drained()
            for j in range(4):
                chans(lambda k: mg[:, k, :], KD, L)
            norm(L)
            for t in range(2):
                for k in range(KD):
                    if t == 0:
                        pe.wait_ge(xh_done, S.next(xh_done))
                    last = nc.tensor.matmul(ps[:, t, 0:36], h[:, k, t * P:t * P + P], rw[:, k, :],
                                            start=(k == 0), stop=(k == KD - 1))
            last.then_inc(rt_p, 1)
            for b in range(4):
                nc.tensor.matmul(ps[:, 4 + b, :], zero[:], x[:, 0, :], start=True, stop=False, skip_group_check=True)
            for g in range(16):
                pe.wait_ge(rt_dg, S.next(rt_dg))
                if g >= 4:
                    pe.wait_ge(rt_wb, S.next(rt_wb))
                nc.tensor.matmul(ps[:, g % 4, :], ones[:], dg[:, g % 2, :, :], start=True, stop=True).then_inc(rt_bc, 1)
            pe.wait_ge(rt_wb, S.next(rt_wb, 4))
            pe.wait_ge(rt_used, S.next(rt_used))
            for t in range(2):
                last = nc.tensor.matmul(ps[:, 0, 0:N_EXP], ones[:], used[:, t, :], start=(t == 0), stop=(t == 1))
            last.then_inc(rt_cnt, 1)

            def gate_up(e):
                for half in range(2):
                    if e is not None:
                        pe.wait_ge(moe_gu, e(half))
                    for which in range(2):
                        n = slab.n
                        full = 16 * (n // SLOTS + 1)
                        s = n % SLOTS
                        pe.wait_ge(slot_full[s], full if slab.i is None
                                   else slab.i * (16 * slab.step // SLOTS) + full)
                        for c in range(2):
                            for k in range(KD):
                                last = nc.tensor.matmul(ps[:, 2 * half + which, c * L:c * L + L],
                                                        ring[:, s, k * 256 + c * P:k * 256 + c * P + P],
                                                        h[:, k, 0:L], start=(k == 0), stop=(k == KD - 1),
                                                        skip_group_check=True)
                        last.then_inc(slab_done, 1)
                        slab.n += 1

            def down(par, ready):
                pe.wait_ge(moe_gu, ready)
                for half in range(2):
                    n = slab.n
                    full = 16 * (n // SLOTS + 1)
                    s = n % SLOTS
                    pe.wait_ge(slot_full[s], full if slab.i is None else slab.i * (16 * slab.step // SLOTS) + full)
                    for c in range(4):
                        for k in range(4):
                            last = nc.tensor.matmul(
                                ps[:, 4 + 2 * half + c // 2, (c % 2) * L:(c % 2) * L + L],
                                ring[:, s, k * 512 + c * P:k * 512 + c * P + P], gu[:, par, k, :],
                                start=False, stop=False, skip_group_check=True)
                    last.then_inc(slab_done, 1)
                    slab.n += 1

            def all_tokens():
                gate_up(None)
                with slabs((N_EXP - 2) // 2, 12) as i:
                    for p in range(2):
                        gate_up(lambda half: i * 4 + (2 * p + half + 1))
                        down(p, i * 4 + (2 * p + 2))
                gate_up(lambda half: 2 * (N_EXP - 2) + half + 1)
                down(0, 2 * (N_EXP - 1))
                down(1, 2 * N_EXP)

            def turn_pick():
                pe.wait_ge(pick_done, S.next(pick_done))
                for t in range(2):
                    last = nc.tensor.transpose(ps[:, 2, t * P:t * P + P], pick_s[:, 0, t * P:t * P + P], ident[:])
                last.then_inc(pick_tp, 1)

            def gather():
                pe.wait_ge(pick_out, S.next(pick_out))
                for k in range(KD):
                    for t in range(2):
                        last = nc.tensor.matmul(psf[:, 1024 + k * P:1024 + k * P + P], ht[:, t, k * P:k * P + P],
                                                pick_t[:, t, :], start=(t == 0), stop=(t == 1), skip_group_check=True)
                    if k % 4 == 3:
                        last.then_inc(hg_pe, 1)

            def gate_up_few(par, between=None):
                for half in range(2):
                    for which in range(2):
                        s = landed()
                        for c in range(2):
                            at = (which * EH + 2 * half + c) * CAP
                            for k in range(KD):
                                last = nc.tensor.matmul(ps[:, par, at:at + CAP],
                                                        ring[:, s, k * 256 + c * P:k * 256 + c * P + P],
                                                        hg[:, k, par * CAP:par * CAP + CAP],
                                                        start=(k == 0), stop=(k == KD - 1), skip_group_check=True)
                        last.then_inc(slab_done, 1)
                    if half == 0 and between:
                        between()

            def down_few(par, gathered=False):
                pe.wait_ge(hv_done, S.next(hv_done))
                for half in range(2):
                    if gathered and half == 0:
                        pe.wait_ge(hg_a, S.next(hg_a))
                    elif gathered:
                        pe.wait_ge(hg_d, S.next(hg_d))
                    s = landed()
                    for k in range(EH):
                        last = nc.tensor.matmul(ps[par * CAP:par * CAP + CAP, 2 + half, :], hv[:, par, k, :],
                                                ring[:, s, k * 512:k * 512 + 512],
                                                start=(k == 0), stop=(k == EH - 1), skip_group_check=True)
                    last.then_inc(slab_done, 1)

            def spread_pair():
                pe.wait_ge(pick_wd, S.next(pick_wd))
                for c in range(KD):
                    if c == 0:
                        pe.wait_ge(yt_a, S.next(yt_a))
                    elif c == 4:
                        pe.wait_ge(yt_d, S.next(yt_d))
                    last = nc.tensor.matmul(ps[:, 4 + c // 2, (c % 2) * L:(c % 2) * L + L], yt[:, c * P:c * P + P],
                                            pick_w[:, 0, :], start=False, stop=False, skip_group_check=True)
                last.then_inc(spread, 1)

            def few_tokens():
                for t in range(2):
                    for k in range(KD):
                        last = nc.tensor.transpose(psf[:, t * D + k * P:t * D + k * P + P], h[:, k, t * P:t * P + P],
                                                   ident[:])
                last.then_inc(ht_tp, 1)
                pe.wait_ge(ht_out, S.next(ht_out))
                turn_pick()
                gather()
                pe.wait_ge(hg_a, S.next(hg_a))
                pe.wait_ge(hg_d, S.next(hg_d))
                gate_up_few(0)
                n0 = slab.n
                with S.loop(N_EXP // 2 - 1, {pick_done: 1, pick_out: 1, hv_done: 2, pick_wd: 1, yt_a: 1, yt_d: 1,
                                             hg_a: 1, hg_d: 1}) as i:
                    slab.step, slab.i = 12, i
                    gate_up_few(1, turn_pick)
                    gather()
                    down_few(0, gathered=True)
                    gate_up_few(0)
                    down_few(1)
                    spread_pair()
                slab.n, slab.step, slab.i = n0 + 12 * (N_EXP // 2 - 1), 0, None
                gate_up_few(1)
                down_few(0)
                down_few(1)
                spread_pair()

            first_slab = slab.n
            pe.wait_ge(rt_max, S.next(rt_max))
            most = pe.value_load(count[0:1, 0:1], min_val=0, max_val=L)
            with pe.If(most > CAP):
                all_tokens()
            with pe.Else():
                slab.n = first_slab
                few_tokens()

        @block.tensor
        def _(pe):
            S = Side(pe)
            slab = Tally()

            def landed():
                n = slab.n
                full = 16 * (n // SLOTS + 1)
                pe.wait_ge(slot_full[n % SLOTS], full if slab.i is None else slab.i * (16 * slab.step // SLOTS) + full)
                slab.n += 1
                return n % SLOTS

            def take():
                if slab.n >= SLOTS:
                    pe.wait_ge(drained, slab.now(SLOTS - 1))
                return landed()

            @contextmanager
            def slabs(trips, per):
                n0 = slab.n
                with pe.Fori(0, trips) as i:
                    slab.step, slab.i = per, i
                    yield i
                slab.n, slab.step, slab.i = n0 + per * trips, 0, None

            def all_drained():
                pe.wait_ge(drained, slab.now())

            def chans(rhs, kn, n, ready=None, k_ready=1):
                s = take()
                for c in range(2):
                    for k in range(kn):
                        if ready is not None and c == 0:
                            pe.wait_ge(ready, S.next(ready, k_ready))
                        last = nc.tensor.matmul(ps[:, 2 * s + c, 0:n], ring[:, s, k * 256 + c * P:k * 256 + c * P + P],
                                                rhs(k), start=(k == 0), stop=(k == kn - 1))
                last.then_inc(slab_done, 1)

            def tokens(lhs, tiles):
                s = take()
                for t in range(tiles):
                    for k in range(KD):
                        last = nc.tensor.matmul(ps[:, 2 * s + t // 2, (t % 2) * 256:(t % 2) * 256 + 256],
                                                lhs(k, t), ring[:, s, k * 256:k * 256 + 256],
                                                start=(k == 0), stop=(k == KD - 1))
                last.then_inc(slab_done, 1)

            def norm(n):
                for k in range(KD):
                    pe.wait_ge(sq_done, S.next(sq_done))
                    last = nc.tensor.matmul(ps[:, 7, 0:n], ones[:], h[:, k, 0:n], start=(k == 0), stop=(k == KD - 1))
                last.then_inc(ssq_done, 1)

            def ffn(n):
                for j in range(4):
                    chans(lambda k: h[:, k, 0:n], KD, n, h_done if j == 0 else None, n // L)
                with slabs(4, 4):
                    for j in range(4):
                        chans(lambda k: h[:, k, 0:n], KD, n)
                for j in range(2):
                    chans(lambda k: h[:, k, 0:n], KD, n)
                all_drained()
                with slabs(2, 8):
                    for pair in range(2):
                        k0 = 0
                        for kn in W2K:
                            s = take()
                            for k in range(kn):
                                for c in range(2):
                                    last = nc.tensor.matmul(
                                        ps[:, 2 * pair + c, 0:n], ring[:, s, k * 256 + c * P:k * 256 + c * P + P],
                                        hid[:, k0 + k, 0:n], start=(k0 + k == 0), stop=(k0 + k == KF - 1))
                            last.then_inc(slab_done, 1)
                            k0 += kn

            def gmlp(l):
                nt = 4 if l == 0 else 2
                pe.wait_ge(gm_v, S.next(gm_v))
                for g in range(4):
                    for t in range(nt):
                        last = nc.tensor.matmul(ps[:, g, t * P:t * P + P], vg[:, t, g * P:g * P + P], ws[:, l, g, :],
                                                start=(t == 0), stop=(t == nt - 1), skip_group_check=True)
                    last.then_inc(gm_sv, 1)

            def gla(l, item0):
                nt = 4 if l == 0 else 2
                item = [item0, item0]
                pe.wait_ge(gm_out, S.next(gm_out))

                def scores(e, d, hh, t):
                    b = item[0] % 2
                    cols = slice(t * P, t * P + P)
                    for lev in range(8):
                        lo, hi = (ex[:, e, lev, cols],) * 2 if lev < 7 else (kk[:, d, hh, cols], qq[:, hh, cols])
                        last = nc.tensor.matmul(ps[:, 2 * b + lev // 4, (lev % 4) * P:(lev % 4) * P + P],
                                                lo, hi, start=(lev % 4 == 0), stop=(lev % 4 == 3),
                                                skip_group_check=True)
                    last.then_inc(sc_done, 1)
                    item[0] += 1

                def values(hh, t):
                    pe.wait_ge(pm_done, S.next(pm_done))
                    for lev in range(8):
                        last = nc.tensor.matmul(ps[:, 4 + hh % 2, t * P:t * P + P], vi[:, t, hh * P:hh * P + P],
                                                pm[:, item[1] % 2, lev, :], start=False, stop=False,
                                                skip_group_check=True)
                    last.then_inc(pv_done, 1)
                    item[1] += 1

                for hh in range(4):
                    if hh >= 2:
                        pe.wait_ge(o_out, S.next(o_out))
                    nc.tensor.matmul(ps[:, 4 + hh % 2, 0:nt * P], zero[:], x[:, 0, 0:nt * P],
                                     start=True, stop=False, skip_group_check=True)
                    for d in range(2):
                        e, order = d, seq[d]
                        pe.wait_ge(xq_done, S.next(xq_done))
                        pe.wait_ge(xk_done, S.next(xk_done))
                        for j in range(3):
                            last = nc.tensor.transpose(ps[:, 6, j * P:j * P + P],
                                                       ex[:, e, 8, order[j] * P:order[j] * P + P], ident[:])
                        last.then_inc(ktp_done, 1)
                        scores(e, d, hh, 0)
                        pe.wait_ge(kt_done, S.next(kt_done))
                        for j in range(3):
                            last = nc.tensor.matmul(ps[:, 7, j * P:j * P + P], kt[:, j, :],
                                                    vi[:, order[j], hh * P:hh * P + P],
                                                    start=(j == 0), stop=(j == 2), skip_group_check=True)
                        last.then_inc(kv_done, 1)
                        for t in range(1, nt):
                            scores(e, d, hh, t)
                            values(hh, t - 1)
                        values(hh, nt - 1)
                        pe.wait_ge(st_done, S.next(st_done))
                        for j in range(1, 4):
                            t = order[j]
                            if t < nt:
                                last = nc.tensor.matmul(ps[:, 4 + hh % 2, t * P:t * P + P], st[:, j - 1, :],
                                                        ex[:, e, 7, t * P:t * P + P], start=False,
                                                        stop=(j == 3 and d == 1), skip_group_check=True)
                        last.then_inc(hd_done, 1)
                pe.wait_ge(o_out, S.next(o_out, 2))
                for hh in range(4):
                    pe.wait_ge(sq_done, S.next(sq_done))
                    nc.tensor.matmul(ps[:, hh, 0:nt * P], ones[:], ex[:, 0, hh, 0:nt * P],
                                     start=True, stop=True).then_inc(ssq_done, 1)
                return item[0]

            pe.wait_ge(const_in, S.next(const_in, 16 * N_CONST))
            pe.wait_ge(zeroed, S.next(zeroed))
            pe.wait_ge(silu_c, S.next(silu_c))
            items = 0
            for l in range(DEPTH):
                n1 = T2 if l == 0 else L
                def rows(first, turned_before=True):
                    for j in range(4):
                        s = landed()
                        if j == 0 and not first:
                            pe.wait_ge(mrow_out, S.next(mrow_out))
                        if j == 3 and turned_before:
                            pe.wait_ge(drained, slab.now(8))
                        for k in range(KD):
                            last = nc.tensor.matmul(ps[0:2, j // 2, (j % 2) * 256:(j % 2) * 256 + 256], cvec[:, k, :],
                                                    ring[:, s, k * 256:k * 256 + 256],
                                                    start=(k == 0), stop=(k == KD - 1), skip_group_check=True)
                        last.then_inc(slab_done, 1)

                def turned():
                    for c in range(8):
                        last = nc.tensor.transpose(ps[:, 2, c * 2:c * 2 + 2], mrow[:, c * P:c * P + P], ident[0:2, 0:2])
                    last.then_inc(mrow_turned, 1)

                if l:
                    all_drained()
                rows(True, False)
                rows(False, False)
                turned()
                n0 = slab.n
                with S.loop(7, {mrow_out: 1}) as i:
                    slab.step, slab.i = 4, i
                    rows(False)
                    turned()
                slab.n, slab.step, slab.i = n0 + 28, 0, None
                pe.wait_ge(mrow_out, S.next(mrow_out))
                pe.wait_ge(drained, slab.now(4))
                turned()
                all_drained()
                norm(T2)
                ffn(T2)
                norm(T2)
                for j in range(14):
                    if j in (4, 5):
                        tokens(lambda k, t: h[:, k, t * P:t * P + P], n1 // P)
                    elif j in (6, 7):
                        tokens(lambda k, t: h[:, k, t * P:t * P + P], 4)
                    else:
                        n = T2 if j < 4 else n1
                        chans(lambda k: h[:, k, 0:n], KD, n, h_done if j == 0 else None, 2)
                gmlp(l)
                items = gla(l, items)
                pe.wait_ge(bo_done, S.next(bo_done))
                for j in range(4):
                    chans(lambda k: h[:, k, 0:n1], KD, n1)
                norm(n1)
                ffn(n1)
            second(pe, S, chans, tokens, all_drained, norm, slabs, landed, slab)

        @block.scalar
        def _(act):
            S = Side(act)
            slab = Tally()

            def own(ins):
                ins.then_inc(act_own, 1)
                act.wait_ge(act_own, S.next(act_own))

            def norm(src, n):
                act.wait_ge(drained, slab.now())
                for k in range(KD):
                    nc.scalar.activation(h[:, k, 0:n], src[:, k, 0:n], ACT.Square).then_inc(sq_done, 1)
                act.wait_ge(inv_done, S.next(inv_done))
                nc.scalar.activation(rs[:, 0:n], rs[:, 0:n], ACT.Sqrt).then_inc(rs_done, 1)

            def modulate(i, n):
                for k in range(KD):
                    act.wait_ge(xh_done, S.next(xh_done))
                    for s, cols in halves(n):
                        nc.scalar.activation(h[:, k, cols], h[:, k, cols], ACT.Identity,
                                             scale=gmod[:, i, k, s:s + 1],
                                             bias=mod[:, 3 * i * KD + k, s:s + 1]).then_inc(h_done, 1)

            def ffn(n):
                def pair(p):
                    s = slab.n % SLOTS
                    act.wait_ge(slab_done, slab.now(-1))
                    act.wait_ge(drained, slab.now(2))
                    nc.scalar.activation(sil[:, p, :, 0:n], ps[:, 2 * s:2 * s + 2, 0:n], ACT.Silu
                                         ).then_inc(silu_done, 1)
                    slab.n += 2
                n0 = slab.n
                with act.Fori(0, 5) as i:
                    slab.step, slab.i = 4, i
                    pair(0)
                    pair(1)
                slab.n, slab.step, slab.i = n0 + 20, 0, None
                pair(0)
                slab.n += 16

            def take(dst, src, func=ACT.Copy):
                act.wait_ge(slab_done, slab.now(-1))
                nc.scalar.activation(dst, src(slab.n % SLOTS), func).then_inc(drained, 1)
                slab.n += 1

            def log1p_exp_neg_abs(t):
                own(nc.scalar.activation(t, t, ACT.Abs))
                own(nc.scalar.activation(t, t, ACT.Exp, scale=-1.0))
                return nc.scalar.activation(t, t, ACT.Ln, bias=1.0)

            def gates(l):
                for d in range(2):
                    if d == 1:
                        act.wait_ge(gate_d, S.next(gate_d))
                    own(nc.scalar.activation(gt1, lf[:, d, :, :], ACT.Abs))
                    own(nc.scalar.activation(gt1, gt1, ACT.Exp, scale=-1.0))
                    nc.scalar.activation(gt1, gt1, ACT.Ln, bias=1.0).then_inc(gate_a, 1)
                    act.wait_ge(gate_d, S.next(gate_d))
                    nc.scalar.activation(kk[:, d, :, :], kk[:, d, :, :], ACT.Exp).then_inc(gate_a, 1)
                    if l == 1:
                        act.wait_ge(gate_d, S.next(gate_d))
                        log1p_exp_neg_abs(gt1).then_inc(gate_a, 1)

            def gla(l):
                nt = 4 if l == 0 else 2
                n = nt * P

                def decays(hd):
                    e = hd % 2
                    act.wait_ge(dec_in, S.next(dec_in))
                    if l == 0:
                        nc.scalar.activation(ex[:, e, :, :], ex[:, e, :, :], ACT.Exp)
                    else:
                        nc.scalar.activation(ex[:, e, 0:8, 0:n], ex[:, e, 0:8, 0:n], ACT.Exp)
                        nc.scalar.activation(ex[:, e, 8, :], ex[:, e, 8, :], ACT.Exp)
                    nc.scalar.activation(eb[:, e, :], be[:, e, :], ACT.Exp).then_inc(dec_out, 1)

                decays(0)
                for hd in range(8):
                    if hd + 1 < 8:
                        decays(hd + 1)
                    act.wait_ge(ktp_done, S.next(ktp_done))
                    nc.scalar.activation(kt[:], ps[:, 6, 0:3 * P], ACT.Copy).then_inc(kt_done, 1)
                    act.wait_ge(hd_done, S.next(hd_done))
                    if hd % 2:
                        hh = hd // 2
                        nc.scalar.activation(h[:, 4 + hh, 0:n], ps[:, 4 + hh % 2, 0:n], ACT.Copy).then_inc(o_out, 1)
                act.wait_ge(o_out, S.next(o_out, 4))
                for hh in range(4):
                    nc.scalar.activation(ex[:, 0, hh, 0:n], h[:, 4 + hh, 0:n], ACT.Square).then_inc(sq_done, 1)
                act.wait_ge(inv_done, S.next(inv_done))
                nc.scalar.activation(ex[:, 0, 4:8, 0:n], ex[:, 0, 4:8, 0:n], ACT.Sqrt).then_inc(rs_done, 1)

            act.dma_start(cvec[:], a["cvec"]).then_inc(const_in, 16)
            act.dma_start(vec[:], a["vec"]).then_inc(const_in, 16)
            act.dma_start(x[:, :, 0:L], a["xin"]).then_inc(const_in, 16)
            act.dma_start(x[:, :, L:T2], a["ctx"]).then_inc(const_in, 16)
            act.dma_start(shaped(work[:, 0:KD * L], KD, L), a["pos"]).then_inc(const_in, 16)
            for dst, name in ((ident, "ident"), (ones, "ones"), (keep, "keep"), (glamask, "glamask"), (ws, "ws"),
                              (blk64, "blk64"), (rot, "rot"), (amask, "amask"), (rw, "rw")):
                act.dma_start(dst[:], a[name]).then_inc(const_in, 16)
            act.dma_start(bs[:].rearrange("p l g t -> p (l g t)"), a["bs"].partition_broadcast(P)).then_inc(const_in, 16)
            act.dma_start(rb[:, 0:36], a["rb"].partition_broadcast(P)).then_inc(const_in, 16)
            act.dma_start(rb[:, 36:44], a["desc"].partition_broadcast(P)).then_inc(const_in, 16)
            act.dma_start(posi[:], a["positions"].partition_broadcast(P)).then_inc(const_in, 16)
            act.wait_ge(const_in, S.next(const_in, 16 * N_CONST))
            nc.scalar.activation(cvec[:], cvec[:], ACT.Silu).then_inc(silu_c, 1)
            act.wait_ge(start_d, S.next(start_d))
            own(nc.scalar.activation(lb1[:, 1], lb1[:, 0], ACT.Abs))
            own(nc.scalar.activation(lb1[:, 1], lb1[:, 1], ACT.Exp, scale=-1.0))
            nc.scalar.activation(lb1[:, 1], lb1[:, 1], ACT.Ln, bias=1.0).then_inc(start_a, 1)
            act.wait_ge(start_d, S.next(start_d))
            nc.scalar.activation(cosn[:], cosn[:], ACT.Sin)
            nc.scalar.activation(sinn[:], sinn[:], ACT.Sin).then_inc(start_a, 1)
            for l in range(DEPTH):
                n1 = T2 if l == 0 else L
                def rows_out():
                    slab.n += 4
                    act.wait_ge(slab_done, slab.now())
                    nc.scalar.activation(mrow, psf[0:2, 0:1024], ACT.Copy).then_inc(mrow_out, 1)

                rows_out()
                n0 = slab.n
                with S.loop(8, {mrow_turned: 1}) as i:
                    slab.step, slab.i = 4, i
                    act.wait_ge(mrow_turned, S.next(mrow_turned))
                    rows_out()
                slab.n, slab.step, slab.i = n0 + 32, 0, None
                act.wait_ge(mrow_turned, S.next(mrow_turned))
                act.wait_ge(mod_done, S.next(mod_done))
                norm(x, T2)
                modulate(0, T2)
                ffn(T2)
                norm(x, T2)
                modulate(1, T2)
                for j in range(14):
                    if j < 4:
                        take(lf[:, j // 2, 2 * (j % 2):2 * (j % 2) + 2, :], lambda s: ps[:, 2 * s:2 * s + 2, :])
                        if j == 3:
                            act.wait_ge(drained, S.next(drained, 0))
                            act.wait_ge(drained, slab.now())
                            gates(l)
                    elif j < 8:
                        nt = 4 if j >= 6 else n1 // P
                        c = (j % 2) * 256
                        dst, func = (vg, ACT.Gelu_apprx_tanh) if j < 6 else (vi, ACT.Copy)
                        take(dst[:, 0:nt, c:c + 256],
                             lambda s: psf[:, s * 1024:s * 1024 + nt * 256].rearrange("p (t c) -> p t c", t=nt), func)
                    else:
                        dst, func = ((qq, ACT.Silu), (uu, ACT.Gelu_apprx_tanh), (og, ACT.Silu))[(j - 8) // 2]
                        c = 2 * (j % 2)
                        take(dst[:, c:c + 2, 0:n1], lambda s: ps[:, 2 * s:2 * s + 2, 0:n1], func)
                act.wait_ge(gm_ms, S.next(gm_ms))
                nc.scalar.activation(vms[:], vms[:], ACT.Sqrt).then_inc(gm_rs, 1)
                gla(l)
                slab.n += 4
                norm(x, n1)
                modulate(2, n1)
                ffn(n1)
            norm(x, L)
            act.wait_ge(xh_done, S.next(xh_done, KD))
            act.wait_ge(mem_in, S.next(mem_in, 16))
            norm(memx, L)
            act.wait_ge(xh_done, S.next(xh_done, KD))
            for j in range(2):
                take(km[:, 2 * j:2 * j + 2, :], lambda s: ps[:, 2 * s:2 * s + 2, 0:L])
            for j in range(2):
                take(vm[:, :, j * 256:j * 256 + 256], lambda s: ps[:, 2 * s, :].rearrange("p (t c) -> p t c", t=2))
            norm(x, L)
            act.wait_ge(xh_done, S.next(xh_done, KD))
            cxf = cx.rearrange("p a b n -> p (a b) n")
            for j in range(20):
                if j < 9:
                    dst = cxf[:, 2 * j:2 * j + 2, :]
                elif j < 15:
                    dst = qk[:, 2 * (j - 9):2 * (j - 9) + 2, :]
                elif j < 18:
                    dst = va[:, :, (j - 15) * 256:(j - 15) * 256 + 256]
                else:
                    dst = qm[:, 2 * (j - 18):2 * (j - 18) + 2, :]
                if 15 <= j < 18:
                    take(dst, lambda s: ps[:, 2 * s, :].rearrange("p (t c) -> p t c", t=2))
                else:
                    take(dst, lambda s: ps[:, 2 * s:2 * s + 2, 0:L])
            n0 = slab.n
            with act.Fori(0, 3) as i:
                slab.step, slab.i = 4, i
                for j in range(4):
                    take(gt[:, bass.ds(i * 8 + 2 * j, 2), :], lambda s: ps[:, 2 * s:2 * s + 2, 0:L], ACT.Sigmoid)
            slab.n, slab.step, slab.i = n0 + 12, 0, None
            act.wait_ge(conv_done, S.next(conv_done))
            act.wait_ge(drained, slab.now())
            nc.scalar.activation(t3, qk, ACT.Square).then_inc(att_a, 1)
            act.wait_ge(att_d, S.next(att_d))
            nc.scalar.activation(t4, t4, ACT.Sqrt).then_inc(att_a, 1)
            act.wait_ge(att_d, S.next(att_d, 2))
            nc.scalar.activation(t3[:, 0:8, :], kqm, ACT.Square).then_inc(att_a, 1)
            act.wait_ge(att_d, S.next(att_d))
            nc.scalar.activation(t4[:, 0:8, :], t4[:, 0:8, :], ACT.Sqrt).then_inc(att_a, 1)

            def exps(u):
                n = 3 * L if units[u][0] == "a" else L
                act.wait_ge(un_mx, S.next(un_mx))
                nc.scalar.activation(sc[:, u % 2, 0:n], sc[:, u % 2, 0:n], ACT.Exp, bias=vms[:, u % 2:u % 2 + 1],
                                     accum_out=vms[:, 2 + u % 2:3 + u % 2]).then_inc(un_ex, 1)

            exps(0)
            for u, (kind, s, t) in enumerate(units):
                if u + 1 < len(units):
                    exps(u + 1)
                n = 3 * L if kind == "a" else L
                act.wait_ge(un_tp, S.next(un_tp))
                nc.scalar.activation(pt[:, u % 2, 0:n], psf[:, 2048:2048 + n], ACT.Copy).then_inc(un_pt, 1)
                act.wait_ge(un_o, S.next(un_o))
                if kind == "a":
                    r = slice(64 * (s % 2), 64 * (s % 2) + 64)
                    nc.scalar.activation(oa[r, s // 2, t * P:t * P + P], ps[r, 6 + u % 2, 0:P], ACT.Copy
                                         ).then_inc(un_out, 1)
                else:
                    nc.scalar.activation(om[:, s, t * P:t * P + P], ps[:, 6 + u % 2, 0:P], ACT.Copy
                                         ).then_inc(un_out, 1)
            slab.n += 16
            norm(x, L)
            act.wait_ge(rt_d, S.next(rt_d))
            nc.scalar.activation(ra[:, 1, :, 0:4], ra[:, 1, :, 0:4], ACT.Exp).then_inc(rt_a, 1)
            act.wait_ge(rt_d, S.next(rt_d))
            nc.scalar.activation(ra[:, 9, :, 0:1], ra[:, 9, :, 0:1], ACT.Exp).then_inc(rt_a, 1)
            for g in range(16):
                act.wait_ge(rt_bc, S.next(rt_bc))
                nc.scalar.activation(wb[:, 2 * g:2 * g + 2, :], ps[:, g % 4, :], ACT.Copy).then_inc(rt_wb, 1)
            def all_tokens():
                for half in range(2):
                    act.wait_ge(slab_done, slab.n + 2 * half + 1)
                    nc.scalar.activation(su[:, half, :, :], ps[:, 2 * half, :], ACT.Silu).then_inc(moe_s, 1)
                with act.Fori(0, N_EXP - 1) as i:
                    for half in range(2):
                        act.wait_ge(slab_done, i * 6 + (slab.n + 4 + 2 * half + 1))
                        act.wait_ge(moe_gu, i * 2 + (half + 1))
                        nc.scalar.activation(su[:, half, :, :], ps[:, 2 * half, :], ACT.Silu).then_inc(moe_s, 1)

            def done(k):
                slab.n += k
                act.wait_ge(slab_done, slab.now())

            def pick_taken():
                act.wait_ge(pick_tp, S.next(pick_tp))
                nc.scalar.activation(pick_t, ps[:, 2, 0:L], ACT.Copy).then_inc(pick_out, 1)

            def gathered():
                act.wait_ge(hg_pe, S.next(hg_pe))
                nc.scalar.activation(hg[:, 0:4, :], ps[:, 2, :], ACT.Copy).then_inc(hg_a, 1)
                S.count(hg_pe)

            def gate_silu(par, first=False):
                done(4)
                if not first:
                    act.wait_ge(hv_done, S.next(hv_done))
                nc.scalar.activation(sg, ps[:, par, 0:EH * CAP], ACT.Silu).then_inc(sg_done, 1)

            def outputs():
                done(1)
                nc.scalar.activation(yt[:, 0:D // 2], ps[:, 2, :], ACT.Copy).then_inc(yt_a, 1)
                slab.n += 1

            def few_tokens():
                act.wait_ge(ht_tp, S.next(ht_tp))
                nc.scalar.activation(ht, psf[:, 0:2 * D], ACT.Copy).then_inc(ht_out, 1)
                pick_taken()
                gathered()
                gate_silu(0, True)
                n0 = slab.n
                with S.loop(N_EXP // 2 - 1, {pick_tp: 1, hg_pe: 2, hv_done: 2}) as i:
                    slab.step, slab.i = 12, i
                    pick_taken()
                    gate_silu(1)
                    gathered()
                    slab.n += 2
                    gate_silu(0)
                    outputs()
                slab.n, slab.step, slab.i = n0 + 12 * (N_EXP // 2 - 1), 0, None
                gate_silu(1)
                slab.n += 2
                outputs()

            act.wait_ge(rt_max, S.next(rt_max))
            most = act.value_load(count[0:1, 0:1], min_val=0, max_val=L)
            with act.If(most > CAP):
                all_tokens()
            with act.Else():
                few_tokens()

        @block.vector
        def _(dve):
            S = Side(dve)
            slab = Tally()

            def own(ins):
                ins.then_inc(dve_own, 1)
                dve.wait_ge(dve_own, S.next(dve_own))

            def tt(o, i0, i1, op):
                return nc.vector.tensor_tensor(o, i0, i1, op)

            def ts(o, i0, s1, s2, op0, op1=ALU.bypass):
                return nc.vector.tensor_scalar(o, i0, s1, s2, op0, op1)

            def stt(o, i0, s, i1, op0, op1):
                return nc.vector.scalar_tensor_tensor(o, i0, s, i1, op0, op1)

            def inv_ms(n):
                dve.wait_ge(ssq_done, S.next(ssq_done))
                own(ts(rs[:, 0:n], ps[:, 7, 0:n], 1.0 / D, EPS, ALU.mult, ALU.add))
                nc.vector.reciprocal(rs[:, 0:n], rs[:, 0:n]).then_inc(inv_done, 1)

            def norm(n):
                inv_ms(n)
                dve.wait_ge(rs_done, S.next(rs_done))
                for k in range(KD):
                    tt(h[:, k, 0:n], x[:, k, 0:n], rs[:, 0:n], ALU.mult).then_inc(xh_done, 1)

            def plain_norm(dst, src, g):
                inv_ms(L)
                dve.wait_ge(rs_done, S.next(rs_done))
                for k in range(KD):
                    stt(dst[:, k, 0:L], src[:, k, 0:L], v(g, k), rs[:, 0:L], ALU.mult, ALU.mult).then_inc(xh_done, 1)

            def residual(chunks, pair, gate, n):
                for c in range(2):
                    for s, cols in halves(n):
                        last = stt(x[:, chunks[c], cols], ps[:, 2 * pair + c, cols], mod[:, gate[c], s:s + 1],
                                   x[:, chunks[c], cols], ALU.mult, ALU.add)
                return last

            def ffn(n, j):
                def pair(p, at):
                    s = slab.n % SLOTS + 1
                    dve.wait_ge(silu_done, S.next(silu_done))
                    dve.wait_ge(slab_done, slab.now(-2))
                    tt(hid[:, at, 0:n], sil[:, p, :, 0:n], ps[:, 2 * s:2 * s + 2, 0:n], ALU.mult).then_inc(drained, 2)
                    slab.n += 2
                n0 = slab.n
                with S.loop(5, {silu_done: 2}) as i:
                    slab.step, slab.i = 4, i
                    pair(0, bass.ds(i * 4, 2))
                    pair(1, bass.ds(i * 4 + 2, 2))
                slab.n, slab.step, slab.i = n0 + 20, 0, None
                pair(0, slice(20, 22))
                for p in range(4):
                    dve.wait_ge(slab_done, slab.now(-4))
                    residual([2 * p, 2 * p + 1], p % 2, [j * KD + 2 * p, j * KD + 2 * p + 1], n).then_inc(drained, 4)
                    slab.n += 4

            def gates(l):
                for d in range(2):
                    f, k = lf[:, d, :, :], kk[:, d, :, :]
                    dve.wait_ge(gate_a, S.next(gate_a))
                    own(stt(gt2, f, 0.0, gt1, ALU.min, ALU.subtract))
                    if l == 0:
                        tt(k, gt2, f, ALU.subtract).then_inc(gate_d, 1)
                        dve.wait_ge(gate_d, S.next(gate_d))
                        own(nc.vector.tensor_copy(f, gt2))
                        dve.wait_ge(gate_a, S.next(gate_a))
                    else:
                        for hh in range(4):
                            last = ts(gt2[:, hh, :], gt2[:, hh, :], lb1[:, 3, d, hh:hh + 1], None, ALU.add)
                        own(last)
                        tt(k, gt2, f, ALU.subtract).then_inc(gate_d, 1)
                        dve.wait_ge(gate_d, S.next(gate_d))
                        for hh in range(4):
                            last = ts(gt1[:, hh, :], gt2[:, hh, :], lb1[:, 2, d, hh:hh + 1], None, ALU.subtract)
                        last.then_inc(gate_d, 1)
                        dve.wait_ge(gate_d, S.next(gate_d))
                        for hh in range(4):
                            last = ts(f[:, hh, :], gt2[:, hh, :], lb1[:, 2, d, hh:hh + 1], None, ALU.max)
                        own(last)
                        dve.wait_ge(gate_a, S.next(gate_a, 2))
                        own(tt(f, f, gt1, ALU.add))
                    if d == 0:
                        nc.vector.memset(be[:, 0, 0:1], 0.0).then_inc(gate_d, 1)
                        dve.wait_ge(gate_d, S.next(gate_d))

            def gmlp(l):
                nt = 4 if l == 0 else 2
                dve.wait_ge(drained, slab.now())
                sq = ex[:, 1, 0:4, :]
                n = nt * 4
                own(tt(sq[:, 0:nt, :], vg[:, 0:nt, :], vg[:, 0:nt, :], ALU.mult))
                own(nc.vector.tensor_reduce(vms[:, 0:n], sq[:, 0:nt, :].rearrange("p t (g c) -> p (t g) c", g=4),
                                            AX, ALU.add))
                own(ts(vms[:, 0:n], vms[:, 0:n], 1.0 / P, EPS, ALU.mult, ALU.add))
                nc.vector.reciprocal(vms[:, 0:n], vms[:, 0:n]).then_inc(gm_ms, 1)
                dve.wait_ge(gm_rs, S.next(gm_rs))
                vv = vg[:, 0:nt, :].rearrange("p t (g c) -> p (t g) c", g=4)
                tt(vv, vv, vms[:, 0:n].unsqueeze(2).to_broadcast([P, n, P]), ALU.mult).then_inc(gm_v, 1)
                for g in range(4):
                    dve.wait_ge(gm_sv, S.next(gm_sv))
                    tl = ex[:, 1, g, 0:nt * P].rearrange("p (t c) -> p t c", t=nt)
                    own(stt(tl, ps[:, g, 0:nt * P].rearrange("p (t c) -> p t c", t=nt), v("g_gmlp", l * 4 + g),
                            bs[:, l, g, :].unsqueeze(1).to_broadcast([P, nt, P]), ALU.mult, ALU.add))
                    last = tt(h[:, g, 0:nt * P], ex[:, 1, g, 0:nt * P], uu[:, g, 0:nt * P], ALU.mult)
                last.then_inc(gm_out, 1)
                dve.wait_ge(gm_out, S.next(gm_out))

            def gla(l, item0):
                nt = 4 if l == 0 else 2
                n = nt * P
                item = [item0]
                sub, add, mul = ALU.subtract, ALU.add, ALU.mult

                def decays(hd):
                    hh, d = divmod(hd, 2)
                    e = hd % 2
                    rev = slice(None, None, -1) if d else slice(None)
                    own(nc.vector.tensor_tensor_scan(bb[:, rev], keep[:], lf[:, d, hh, :][:, rev], 0.0, mul, add))
                    b64 = blocks(bb, 64)
                    early, late = early_late(b64, d)
                    ends = 63 * (1 - d)
                    ee, le = early[:, :, ends:ends + 1], late[:, :, ends:ends + 1]
                    if hd >= 2:
                        dve.wait_ge(hd_done, S.tally(hd_done).n + hd - 1)
                    own(tt(be[:, e, :], ee.squeeze(2), le.squeeze(2), add))
                    for lev in range(6):
                        m = 1 << lev
                        nb = n // (2 * m)
                        src_e, src_l = early_late(blocks(bb[:, 0:n], m), d)
                        dst_e, dst_l = early_late(blocks(ex[:, e, lev, 0:n], m), d)
                        at = (m - 1) * (1 - d)
                        ref = src_e[:, :, at:at + 1].to_broadcast([P, nb, m])
                        tt(dst_l, src_l, ref, sub)
                        tt(dst_e, ref, src_e, sub)
                    e6, l6 = early_late(blocks(ex[:, e, 6, 0:n], 64), d)
                    e7, l7 = early_late(blocks(ex[:, e, 7, 0:n], 64), d)
                    e8, l8 = early_late(blocks(ex[:, e, 8, :], 64), d)
                    eeb = ee.to_broadcast([P, 4, 64])
                    nc.vector.tensor_copy(l6, late[:, 0:nt])
                    tt(e6, eeb[:, 0:nt], early[:, 0:nt], sub)
                    nc.vector.tensor_copy(e7, early[:, 0:nt])
                    tt(l7, late[:, 0:nt], eeb[:, 0:nt], add)
                    tt(l8, le.to_broadcast([P, 4, 64]), late, sub)
                    tt(e8, be[:, e, :].unsqueeze(2).to_broadcast([P, 4, 64]), early, sub).then_inc(dec_in, 1)

                def times_q(hd):
                    hh, d = divmod(hd, 2)
                    e = hd % 2
                    dve.wait_ge(dec_out, S.next(dec_out))
                    for lev in range(7):
                        m = 1 << lev
                        _, late = early_late(blocks(ex[:, e, lev, 0:n], m), d)
                        _, ql = early_late(blocks(qq[:, hh, 0:n], m), d)
                        tt(late, late, ql, mul)
                    tt(ex[:, e, 7, 0:n], ex[:, e, 7, 0:n], qq[:, hh, 0:n], mul).then_inc(xq_done, 1)

                def mask(hd):
                    dve.wait_ge(sc_done, S.next(sc_done))
                    if item[0] >= 2:
                        dve.wait_ge(pv_done, item[0] - 1)
                    b = item[0] % 2
                    tt(pm[:, b, :, :], psf[:, b * 1024:b * 1024 + 1024].rearrange("p (v t) -> p v t", v=8),
                       gm[:, hd % 2, :, :], mul).then_inc(pm_done, 1)
                    item[0] += 1

                def states(hd):
                    e = hd % 2
                    order = seq[hd % 2]
                    dve.wait_ge(kv_done, S.next(kv_done))
                    if hd >= 1:
                        dve.wait_ge(hd_done, S.tally(hd_done).n + hd)
                    own(nc.vector.tensor_copy(st[:, 0, :], ps[:, 7, 0:P]))
                    own(stt(st[:, 1, :], st[:, 0, :], eb[:, e, order[1]:order[1] + 1], ps[:, 7, P:2 * P], mul, add))
                    stt(st[:, 2, :], st[:, 1, :], eb[:, e, order[2]:order[2] + 1], ps[:, 7, 2 * P:3 * P], mul, add
                        ).then_inc(st_done, 1)

                decays(0)
                times_q(0)
                for hd in range(8):
                    if hd + 1 < 8:
                        decays(hd + 1)
                    mask(hd)
                    states(hd)
                    mask(hd)
                    if hd + 1 < 8:
                        times_q(hd + 1)
                    for t in range(2, nt):
                        mask(hd)
                S.count(hd_done, 8)
                dve.wait_ge(o_out, S.next(o_out, 4))
                dve.wait_ge(ssq_done, S.next(ssq_done, 4))
                r4 = ex[:, 0, 4:8, 0:n]
                own(ts(r4, ps[:, 0:4, 0:n], 1.0 / P, EPS, mul, add))
                nc.vector.reciprocal(r4, r4).then_inc(inv_done, 1)
                dve.wait_ge(rs_done, S.next(rs_done))
                for hh in range(4):
                    own(stt(h[:, 4 + hh, 0:n], h[:, 4 + hh, 0:n], v("g_hgrn", l * 4 + hh), r4[:, hh, :], mul, mul))
                tt(h[:, 4:8, 0:n], h[:, 4:8, 0:n], og[:, :, 0:n], mul).then_inc(bo_done, 1)
                return item[0]

            nc.vector.memset(zero[:], 0.0).then_inc(zeroed, 1)
            nc.vector.memset(vms[:], 1.0)
            nc.vector.memset(work[:, WORK - 2 * T2:WORK], 0.0)
            dve.wait_ge(const_in, S.next(const_in, 16 * N_CONST))
            lb = v("lb", 0, 16).rearrange("p (d l c) -> p d l c", d=2, l=2)
            tt(lb1[:, 0], lb[:, :, 1, :], lb[:, :, 0, :], ALU.subtract).then_inc(start_d, 1)
            dve.wait_ge(start_d, S.next(start_d))
            dve.wait_ge(start_a, S.next(start_a))
            stt(lb1[:, 2], lb1[:, 0], 0.0, lb1[:, 1], ALU.min, ALU.subtract)
            own(ts(lb1[:, 3], lb1[:, 0], -1.0, 0.0, ALU.mult, ALU.min))
            own(tt(lb1[:, 3], lb1[:, 3], lb1[:, 1], ALU.subtract))
            ang, rnd = bb[:, 0:L], bb[:, L:T2]
            own(nc.vector.tensor_copy(ang, posi[:]))
            own(ts(ang, ang, v("inv"), None, ALU.mult))
            for dst, quarter in ((sinn, 0.0), (cosn, 0.25)):
                own(ts(rnd, ang, 1.0 / TWO_PI, quarter, ALU.mult, ALU.add))
                own(ts(rnd, rnd, ROUND, None, ALU.add))
                own(ts(rnd, rnd, ROUND, None, ALU.subtract))
                own(stt(dst[:], rnd, -PI_1, ang, ALU.mult, ALU.add))
                own(stt(dst[:], rnd, -PI_2, dst[:], ALU.mult, ALU.add))
                own(stt(dst[:], rnd, -PI_3, dst[:], ALU.mult, ALU.add))
                own(ts(dst[:], dst[:], quarter * TWO_PI, PI_MAX, ALU.add, ALU.min))
                own(ts(dst[:], dst[:], -PI_MAX, None, ALU.max))
            tt(x[:, :, 0:L], x[:, :, 0:L], shaped(work[:, 0:KD * L], KD, L), ALU.add).then_inc(start_d, 1)
            dve.wait_ge(start_d, S.next(start_d))
            dve.wait_ge(start_a, S.next(start_a))
            items = 0
            for l in range(DEPTH):
                n1 = T2 if l == 0 else L
                b0 = VEC["b_ada"][0] + l * N_MOD * KD
                with S.loop(9, {mrow_turned: 1}) as i:
                    dve.wait_ge(mrow_turned, S.next(mrow_turned))
                    tt(mod[:, bass.ds(i * 8, 8), :], ps[:, 2, 0:16].rearrange("p (c r) -> p c r", c=8),
                       vec[:, bass.ds(i * 8 + b0, 8)].unsqueeze(2).to_broadcast([P, 8, 2]), ALU.add
                       ).then_inc(drained, 4)
                slab.n += 36
                dve.wait_ge(drained, slab.now())
                for i in range(3):
                    stt(gmod[:, i], mod[:, (3 * i + 1) * KD:(3 * i + 2) * KD, :], 1.0,
                        v("g_norm", (l * 3 + i) * KD, KD).unsqueeze(2).to_broadcast([P, KD, 2]), ALU.add, ALU.mult)
                for i in (2, 8):
                    g = mod[:, i * KD:(i + 1) * KD, :]
                    last = ts(g, g, 0.5, None, ALU.mult)
                last.then_inc(mod_done, 1)
                dve.wait_ge(mod_done, S.next(mod_done))
                norm(T2)
                ffn(T2, 2)
                norm(T2)
                gates(l)
                slab.n += 14
                gmlp(l)
                items = gla(l, items)
                for j in range(4):
                    s = slab.n % SLOTS
                    dve.wait_ge(slab_done, slab.now(-1))
                    residual([2 * j, 2 * j + 1], s, [5 * KD + 2 * j, 5 * KD + 2 * j + 1], n1).then_inc(drained, 1)
                    slab.n += 1
                norm(n1)
                ffn(n1, 8)
            plain_norm(x, x, "g_final")
            dve.wait_ge(mem_in, S.next(mem_in, 16))
            plain_norm(h, memx, "g_mem")
            slab.n += 4
            plain_norm(h, x, "g_mix")
            slab.n += 9
            dve.wait_ge(drained, slab.now())
            u, w = cx[:, 0], cx[:, 2]
            own(tt(u, w, u, ALU.mult))
            for c in range(6):
                own(ts(w[:, c, :], u[:, c, :], v("w_conv", 6 + c), None, ALU.mult))
                own(stt(w[:, c, 1:L], u[:, c, 0:L - 1], v("w_conv", c), w[:, c, 1:L], ALU.mult, ALU.add))
                own(stt(w[:, c, 0:L - 1], u[:, c, 1:L], v("w_conv", 12 + c), w[:, c, 0:L - 1], ALU.mult, ALU.add))
            tt(zc, w, cx[:, 1], ALU.mult).then_inc(conv_done, 1)
            dve.wait_ge(conv_done, S.next(conv_done))
            slab.n += 23
            dve.wait_ge(att_p, S.next(att_p))
            own(ts(t4, psf[:, 0:AH * L].rearrange("p (c n) -> p c n", c=AH), 1.0 / 64, EPS, ALU.mult, ALU.add))
            nc.vector.reciprocal(t4, t4).then_inc(att_d, 1)
            dve.wait_ge(att_a, S.next(att_a, 2))
            stt(qk[:, 0:6, :], qk[:, 0:6, :], v("g_qa"), t4[:, 0:6, :], ALU.mult, ALU.mult)
            stt(qk[:, 6:12, :], qk[:, 6:12, :], v("g_ka"), t4[:, 6:12, :], ALU.mult, ALU.mult).then_inc(att_d, 1)
            dve.wait_ge(att_d, S.next(att_d, 2))
            dve.wait_ge(att_p, S.next(att_p))
            tt(t3, psf[:, 0:AH * L].rearrange("p (c n) -> p c n", c=AH),
               sinn[:].unsqueeze(1).to_broadcast([P, AH, L]), ALU.mult)
            own(tt(qk, qk, cosn[:].unsqueeze(1).to_broadcast([P, AH, L]), ALU.mult))
            tt(qk, qk, t3, ALU.add).then_inc(att_d, 1)
            dve.wait_ge(att_p, S.next(att_p))
            own(ts(t4[:, 0:8, :], psf[:, 0:8 * L].rearrange("p (c n) -> p c n", c=8), 1.0 / P, EPS,
                   ALU.mult, ALU.add))
            nc.vector.reciprocal(t4[:, 0:8, :], t4[:, 0:8, :]).then_inc(att_d, 1)
            dve.wait_ge(att_a, S.next(att_a, 2))
            stt(km, km, v("g_km"), t4[:, 0:4, :], ALU.mult, ALU.mult)
            stt(qm, qm, v("g_qm"), t4[:, 4:8, :], ALU.mult, ALU.mult).then_inc(att_d, 1)

            def scaled(u):
                kind, s, t = units[u]
                e = u % 2
                n = 3 * L if kind == "a" else L
                dve.wait_ge(un_sc, S.next(un_sc))
                if u >= 2:
                    dve.wait_ge(un_tp, S.next(un_tp))
                src = psf[:, e * 1024:e * 1024 + n]
                if kind == "a":
                    own(stt(sc[:, e, 0:n], src, 64 ** -0.5, amask[:, t, :], ALU.mult, ALU.add))
                else:
                    own(ts(sc[:, e, 0:n], src, P ** -0.5, None, ALU.mult))
                own(nc.vector.reduce_max(vms[:, 4 + e:5 + e], sc[:, e, 0:n], AX))
                ts(vms[:, e:e + 1], vms[:, 4 + e:5 + e], -1.0, None, ALU.mult).then_inc(un_mx, 1)

            scaled(0)
            for u, (kind, s, t) in enumerate(units):
                if u + 1 < len(units):
                    scaled(u + 1)
                e = u % 2
                n = 3 * L if kind == "a" else L
                dve.wait_ge(un_ex, S.next(un_ex))
                own(nc.vector.reciprocal(vms[:, 6 + e:7 + e], vms[:, 2 + e:3 + e]))
                ts(sc[:, e, 0:n], sc[:, e, 0:n], vms[:, 6 + e:7 + e], None, ALU.mult).then_inc(un_pr, 1)
            for br in range(3):
                for j in range(4):
                    s = slab.n % SLOTS
                    dve.wait_ge(slab_done, slab.now(-1))
                    g = gt[:, br * KD + 2 * j:br * KD + 2 * j + 2, :]
                    m = mg[:, 2 * j:2 * j + 2, :]
                    if br == 0:
                        tt(m, g, ps[:, 2 * s:2 * s + 2, 0:L], ALU.mult).then_inc(drained, 1)
                    else:
                        dve.wait_ge(drained, slab.now(1))
                        tmp = t3[:, 2 * (j % 2):2 * (j % 2) + 2, :]
                        own(tt(tmp, g, ps[:, 2 * s:2 * s + 2, 0:L], ALU.mult))
                        tt(m, m, tmp, ALU.add).then_inc(drained, 1)
                    slab.n += 1
            for j in range(4):
                s = slab.n % SLOTS
                dve.wait_ge(slab_done, slab.now(-1))
                xc = x[:, 2 * j:2 * j + 2, 0:L]
                tt(xc, xc, ps[:, 2 * s:2 * s + 2, 0:L], ALU.add).then_inc(drained, 1)
                slab.n += 1
            plain_norm(h, x, "g_ffn")
            dve.wait_ge(rt_p, S.next(rt_p))
            own(tt(lg[:], ps[:, 0:2, 0:36], rb[:, 0:36].unsqueeze(1).to_broadcast([P, 2, 36]), ALU.add))
            gl = lg[:, :, 0:4]
            el = lg[:, :, 4:36].rearrange("p t (g e) -> p t g e", g=4)

            def wide(col, n):
                return col.to_broadcast([P, 2, n])

            def one_hot(dst, src, top, n):
                own(nc.vector.tensor_reduce(top, src, AX, ALU.max))
                own(tt(dst, src, wide(top, n), ALU.is_equal))
                own(tt(dst, dst, rb[:, 36:36 + n].unsqueeze(1).to_broadcast([P, 2, n]), ALU.mult))
                own(nc.vector.tensor_reduce(ra[:, 10, :, 0:1], dst, AX, ALU.max))
                own(tt(dst, dst, wide(ra[:, 10, :, 0:1], n), ALU.is_equal))

            gm1, goh, tmp = ra[:, 0, :, 0:1], ra[:, 2, :, 0:4], ra[:, 3]
            one_hot(goh, gl, gm1, 4)
            tt(ra[:, 1, :, 0:4], gl, wide(gm1, 4), ALU.subtract).then_inc(rt_d, 1)
            dve.wait_ge(rt_d, S.next(rt_d))
            sel = ra[:, 4]
            own(tt(sel, el[:, :, 0, :], wide(goh[:, :, 0:1], 8), ALU.mult))
            for g in range(1, 4):
                own(tt(tmp, el[:, :, g, :], wide(goh[:, :, g:g + 1], 8), ALU.mult))
                own(tt(sel, sel, tmp, ALU.add))
            m1, m2, o1, o2 = ra[:, 5, :, 0:1], ra[:, 6, :, 0:1], ra[:, 7], ra[:, 8]
            one_hot(o1, sel, m1, 8)
            own(stt(tmp, o1, -3e38, sel, ALU.mult, ALU.add))
            one_hot(o2, tmp, m2, 8)
            e2 = ra[:, 9, :, 0:1]
            tt(e2, m2, m1, ALU.subtract).then_inc(rt_d, 1)
            dve.wait_ge(rt_a, S.next(rt_a, 2))
            z, w1, w2 = ra[:, 11, :, 0:1], ra[:, 11, :, 1:2], ra[:, 11, :, 2:3]
            own(nc.vector.tensor_reduce(z, ra[:, 1, :, 0:4], AX, ALU.add))
            own(stt(w1, e2, 1.0, z, ALU.add, ALU.mult))
            own(nc.vector.reciprocal(w1, w1))
            own(tt(w2, w1, e2, ALU.mult))
            own(tt(o1, o1, wide(w1, 8), ALU.mult))
            own(tt(o2, o2, wide(w2, 8), ALU.mult))
            own(tt(o1, o1, o2, ALU.add))
            for g in range(4):
                last = tt(rwt[:, :, g * 8:g * 8 + 8], o1, wide(goh[:, :, g:g + 1], 8), ALU.mult)
            own(last)
            ts(used, rwt, 0.0, None, ALU.is_gt).then_inc(rt_used, 1)
            for g in range(16):
                if g >= 2:
                    dve.wait_ge(rt_bc, S.next(rt_bc))
                for j in range(4):
                    e, t = 2 * g + j // 2, j % 2
                    last = ts(dg[:, g % 2, j, :], ident[:], rwt[:, t, e:e + 1], None, ALU.mult)
                last.then_inc(rt_dg, 1)
            dve.wait_ge(rt_wb, S.next(rt_wb, 16))
            dve.wait_ge(rt_cnt, S.next(rt_cnt))
            own(nc.vector.tensor_reduce(top, ps[:, 0, 0:N_EXP], AX, ALU.max))
            nc.vector.tensor_copy(count, top).then_inc(rt_max, 1)
            dve.wait_ge(rt_max, S.next(rt_max))

            def hidden(par, e, half, s_ready, slabs_ready):
                dve.wait_ge(moe_s, s_ready)
                own(tt(tt2[:, half, :, :], su[:, half, :, :], wb[:, e, :].to_broadcast([P, 2, L]), ALU.mult))
                dve.wait_ge(slab_done, slabs_ready)
                tt(gu[:, par, 2 * half:2 * half + 2, :], tt2[:, half, :, :],
                   ps[:, 2 * half + 1, :].rearrange("p (c n) -> p c n", c=2), ALU.mult).then_inc(moe_gu, 1)

            def all_tokens():
                for half in range(2):
                    hidden(0, slice(0, 1), half, half + 1, slab.n + 2 * half + 2)
                own_steps = {dve_own: 4}
                with S.loop((N_EXP - 2) // 2, own_steps) as i:
                    for p in range(2):
                        for half in range(2):
                            hidden(1 - p, bass.ds(i * 2 + (1 + p), 1), half, i * 4 + (2 + 2 * p + half + 1),
                                   i * 12 + (slab.n + 4 + 6 * p + 2 * half + 2))
                for half in range(2):
                    hidden(1, slice(N_EXP - 1, N_EXP), half, 2 * (N_EXP - 1) + half + 1,
                           slab.n + 4 + 6 * (N_EXP - 2) + 2 * half + 2)
                dve.wait_ge(slab_done, slab.n + 6 * N_EXP)

            def pick(e, first=False):
                for half in range(2):
                    r = slice(half * CAP, half * CAP + CAP)
                    last = ts(taken[r], wb[r, e(half), :], 0.0, None, ALU.is_gt)
                own(last)
                own(nc.vector.tensor_tensor_scan(rank[:, 0, :], taken[:, 0, :], taken[:, 0, :], 0.0, ALU.add, ALU.max))
                own(tt(rank, rank, taken, ALU.mult))
                if not first:
                    dve.wait_ge(pick_tp, S.next(pick_tp))
                ts(pick_s, rank, v("slot"), None, ALU.is_equal).then_inc(pick_done, 1)
                dve.wait_ge(pick_done, S.next(pick_done))

            def weigh(e):
                for half in range(2):
                    r = slice(half * CAP, half * CAP + CAP)
                    last = tt(pick_w[r], pick_s[r], wb[r, e(half), :], ALU.mult)
                last.then_inc(pick_wd, 1)

            def hidden_few(par):
                dve.wait_ge(sg_done, S.next(sg_done))
                tt(hv[:, par, :, :], sg, ps[:, par, EH * CAP:2 * EH * CAP].rearrange("p (c n) -> p c n", c=EH), ALU.mult
                   ).then_inc(hv_done, 1)

            def gathered():
                dve.wait_ge(hg_pe, S.next(hg_pe, 2))
                nc.vector.tensor_copy(hg[:, 4:8, :], ps[:, 3, :].rearrange("p (c n) -> p c n", c=4)).then_inc(hg_d, 1)

            def outputs(k):
                slab.n += k
                dve.wait_ge(slab_done, slab.now())
                nc.vector.tensor_copy(yt[:, D // 2:D], ps[:, 3, :]).then_inc(yt_d, 1)
                dve.wait_ge(spread, S.next(spread))

            def few_tokens():
                pick(lambda half: slice(half, half + 1), True)
                weigh(lambda half: slice(half, half + 1))
                gathered()
                hidden_few(0)
                slab.n += 4
                n0 = slab.n
                with S.loop(N_EXP // 2 - 1, {dve_own: 3, pick_tp: 1, pick_done: 1, sg_done: 2, spread: 1, hg_pe: 2}) as i:
                    slab.step, slab.i = 12, i
                    following = lambda half: bass.ds(i * 2 + (2 + half), 1)
                    pick(following)
                    hidden_few(1)
                    gathered()
                    hidden_few(0)
                    outputs(12)
                    weigh(following)
                slab.n, slab.step, slab.i = n0 + 12 * (N_EXP // 2 - 1), 0, None
                hidden_few(1)
                outputs(8)

            most = dve.value_load(count[0:1, 0:1], min_val=0, max_val=L)
            own_before = S.tally(dve_own).n
            with dve.If(most > CAP):
                all_tokens()
            with dve.Else():
                S.tally(dve_own).n = own_before
                few_tokens()
            tt(x[:, :, 0:L], x[:, :, 0:L], psf[:, 2048:4096].rearrange("p (c n) -> p c n", c=KD), ALU.add
               ).then_inc(fin, 1)
        @block.gpsimd
        def _(pool):
            S = Side(pool)
            for l in range(DEPTH):
                n = T2 if l == 0 else L
                for hd in range(8):
                    hh, d = divmod(hd, 2)
                    e = hd % 2
                    pool.wait_ge(dec_out, S.next(dec_out))
                    for lev in range(7):
                        m = 1 << lev
                        early, _ = early_late(blocks(ex[:, e, lev, 0:n], m), d)
                        ke, _ = early_late(blocks(kk[:, d, hh, 0:n], m), d)
                        nc.gpsimd.tensor_tensor(early, early, ke, ALU.mult)
                    nc.gpsimd.tensor_tensor(ex[:, e, 8, :], ex[:, e, 8, :], kk[:, d, hh, :], ALU.mult
                                            ).then_inc(xk_done, 1)
_OUT = (P, KD, L)


def slabs_of(w, cols=256):
    k, n = w.shape
    return w.reshape(k // P, P, n // cols, cols).transpose(2, 1, 0, 3).reshape(n // cols, P, -1)


def chans_of(w):
    return w.reshape(-1, P).T


def constants():
    f = np.float32
    rows = np.repeat(np.arange(L // 64), 64).astype(f)
    cols = np.tile(np.arange(64), L // 64).astype(f)
    freq = (f(10000.0) ** (-np.arange(256, dtype=f) / f(256))).astype(f)
    emb = []
    for p in (rows, cols):
        ang = p[:, None] * freq[None, :]
        emb += [np.sin(ang), np.cos(ang)]
    pos = np.concatenate(emb, axis=-1).astype(f)
    c = {"pos": np.ascontiguousarray(pos.T.reshape(KD, P, L).transpose(1, 0, 2))}
    c["ident"] = np.eye(P, dtype=f)
    c["slot"] = (np.arange(P) % CAP + 1).astype(f).reshape(P, 1)
    c["ones"] = np.ones((P, P), f)
    c["keep"] = np.ascontiguousarray(np.broadcast_to((np.arange(T2) % 64 != 0).astype(f), (P, T2)))
    s, t = np.arange(P)[:, None], np.arange(P)[None, :]
    m = np.zeros((P, 2, 8, P), f)
    for lev in range(LEVELS):
        size = 1 << lev
        same = (s // (2 * size)) == (t // (2 * size))
        m[:, 0, lev] = same & (s // size % 2 == 0) & (t // size % 2 == 1)
        m[:, 1, lev] = same & (s // size % 2 == 1) & (t // size % 2 == 0)
    m[:, :, 7] = (s == t)[:, None, :]
    c["glamask"] = m.reshape(P, -1)
    c["blk64"] = (s // 64 == t // 64).astype(f)
    r = np.zeros((P, P), f)
    for b in (0, 64):
        for i in range(8):
            r[b + 8 + i, b + i] = -1
            r[b + i, b + 8 + i] = 1
    c["rot"] = r
    i, j = np.arange(L)[:, None], np.arange(L)[None, :]
    masks = []
    for window, dil in ((128, 1), (512, 4), (2048, 16)):
        ok = (i % dil == j % dil) & (np.abs(i - j) // dil <= window // (2 * dil))
        masks.append(np.where(ok, f(0), f(NEG)))
    c["amask"] = np.ascontiguousarray(np.concatenate(masks, 1).astype(f).reshape(2, P, 3 * L).transpose(1, 0, 2))
    c["desc"] = np.arange(8, 0, -1).astype(f)
    return c


def layout(inp):
    a = dict(constants())
    A = {k: np.asarray(val) for k, val in inp.items()}
    cat = np.concatenate
    a["cvec"] = np.stack([A["c"][0], A["c_ctx"]], -1).reshape(KD, P, 2).transpose(1, 0, 2)
    for name, src in (("xin", A["x"][0]), ("ctx", A["ctx"][0]), ("memx", A["mem_2"][0])):
        a[name] = src.T.reshape(KD, P, L).transpose(1, 0, 2)
    inv = np.zeros((P, 1), np.float32)
    f = (np.float32(500000.0) ** (-np.arange(0, 16, 2, dtype=np.float32) / np.float32(16))).astype(np.float32)
    for b in (0, 8, 64, 72):
        inv[b:b + 8, 0] = f
    two = lambda g: np.tile(g.reshape(-1), 2).reshape(P, 1)
    cols = {
        "b_ada": chans_of(A["b_ada"]),
        "g_norm": cat([chans_of(A[n][l]) for l in range(DEPTH) for n in ("norm_ffn1_g", "norm_mix_g", "norm_ffn2_g")], 1),
        "g_gmlp": chans_of(A["gmlp_norm_g"]),
        "lb": cat([chans_of(A["hgrn_lb_fwd"]), chans_of(A["hgrn_lb_bwd"])], 1),
        "g_hgrn": chans_of(A["hgrn_norm_g"]), "g_final": chans_of(A["norm_final_g"]),
        "g_mix": chans_of(A["g_mix_2"]), "g_mem": chans_of(A["g_mem_2"]),
        "g_qa": two(A["g_qn_attn_2"]), "g_ka": two(A["g_kn_attn_2"]),
        "w_conv": chans_of(A["w_conv_2"]), "g_qm": A["g_qn_mem_2"].reshape(P, 1), "g_km": A["g_kn_mem_2"].reshape(P, 1),
        "g_ffn": chans_of(A["g_ffn_2"]), "inv": inv, "slot": a.pop("slot")}
    a["vec"] = cat([cols[n] for n in VEC], 1)
    a["ws"] = A["gmlp_ws"].transpose(3, 0, 1, 2)
    a["bs"] = A["gmlp_bs"].reshape(-1)
    a["rb"] = cat([A["b_router_group_2"].reshape(-1), A["b_router_expert_2"].reshape(-1)])
    a["rw"] = cat([A["w_router_group_2"][0], A["w_router_expert_2"][0]], 1).reshape(KD, P, 36).transpose(1, 0, 2)
    a["positions"] = A["positions_2"].reshape(-1)
    a["w_ada"] = cat([slabs_of(A["w_ada"][l]) for l in range(DEPTH)])
    a["w13"] = cat([np.stack([slabs_of(A[f"ffn{i}_w1"][l]), slabs_of(A[f"ffn{i}_w3"][l])], 1).reshape(22, P, SLAB)
                    for l in range(DEPTH) for i in (1, 2)])
    a["w2"] = cat([slabs_of(A[f"ffn{i}_w2"][l]) for l in range(DEPTH) for i in (1, 2)])
    order = [6, 7, 8, 9, 2, 3, 10, 11, 4, 5, 0, 1, 12, 13]
    a["w_in"] = cat([slabs_of(A["w_in"][l])[order] for l in range(DEPTH)])
    a["w_out"] = cat([slabs_of(A["w_out"][l]) for l in range(DEPTH)])
    a["w_mem"] = slabs_of(A["w_mem_kv_2"][0])
    order = list(range(9, 18)) + list(range(0, 9)) + list(range(18, 32))
    a["w_in2"] = slabs_of(A["w_in_2"][0])[order]
    a["w_pa"], a["w_pc"], a["w_pm"], a["w_out2"] = (slabs_of(A[n][0]) for n in (
        "w_proj_attn_2", "w_proj_conv_2", "w_proj_mem_2", "w_out_2"))
    gu, dn = [], []
    for e in range(N_EXP):
        g, u = slabs_of(A["w_gate_2"][0, e]), slabs_of(A["w_up_2"][0, e])
        gu.append([g[0], u[0], g[1], u[1]])
        dn.append(list(slabs_of(A["w_down_2"][0, e], 512)))
    moe = list(gu[0])
    for e in range(1, N_EXP):
        moe += gu[e] + dn[e - 1]
    a["w_moe"] = np.stack(moe + dn[-1])
    return {k: np.ascontiguousarray(val) for k, val in a.items()}


def kernel(**inputs):
    import concourse.bacc as bacc
    from concourse.bass_utils import run_bass_kernel_spmd

    nc = bacc.Bacc("TRN2", target_bir_lowering=False, num_devices=1)
    arrays = layout(inputs)
    aps = {n: nc.dram_tensor(f"in_{n}", arr.shape, mybir.dt.from_np(arr.dtype), kind="ExternalInput").ap()
           for n, arr in arrays.items()}
    out = nc.dram_tensor("result", _OUT, F32, kind="ExternalOutput").ap()
    build(nc, aps, out)
    r = run_bass_kernel_spmd(nc, [{f"in_{n}": arr for n, arr in arrays.items()}], core_ids=[0])
    got = r.results[0]["result"]
    return np.ascontiguousarray(got.transpose(1, 0, 2).reshape(D, L).T).reshape(1, L, D)
```
